# Optimizing a Trainium2 kernel written in Bass

```python
import jax, jax.numpy as jnp
from jax import lax
import numpy as np

D_MODEL = 1024
BATCH = 1
SEQ = 512
DEPTH = 1

CHUNK = 64
EPS = 1e-6
ROPE_THETA = 10000.0
NEG_INF = -1e30

ATT_HEADS = 8
ATT_KV_HEADS = 2
ATT_HEAD_DIM = D_MODEL // ATT_HEADS
WINDOW = 128
WINDOW_CHUNKS = WINDOW // CHUNK

RET_HEADS = D_MODEL // 256
RET_QK_DIM = 256
RET_V_DIM = 512

PEER_HEADS = 8
N_KEYS = 128
N_EXPERTS = N_KEYS * N_KEYS
PEER_QUERY_DIM = 256
PEER_TOPK = 16
PEER_TOKEN_BLOCK = 128

PLE_DIM = 256

ATT_Q_W = ATT_HEADS * ATT_HEAD_DIM
ATT_KV_W = ATT_KV_HEADS * ATT_HEAD_DIM
RET_QK_W = RET_HEADS * RET_QK_DIM
RET_V_W = RET_HEADS * RET_V_DIM
IN_SPLITS = (ATT_Q_W, ATT_KV_W, ATT_KV_W, RET_QK_W, RET_QK_W, RET_V_W, RET_V_W, D_MODEL, D_MODEL)
IN_W = sum(IN_SPLITS)

kernel_name = "hybrid_swa_retention_peer_block"

def rms_norm(x, g):
    xf = x.astype(jnp.float32)
    y = xf * lax.rsqrt(jnp.mean(xf * xf, axis=-1, keepdims=True) + EPS)
    return (y * g.astype(jnp.float32)).astype(x.dtype)

def rope_tables(seq, dim):
    inv = 1.0 / (ROPE_THETA ** (jnp.arange(0, dim, 2, dtype=jnp.float32) / dim))
    ang = jnp.arange(seq, dtype=jnp.float32)[:, None] * inv[None, :]
    return jnp.cos(ang), jnp.sin(ang)

def apply_rope(t, cos, sin):
    t1, t2 = jnp.split(t.astype(jnp.float32), 2, axis=-1)
    c = cos[None, :, None, :]
    s = sin[None, :, None, :]
    return jnp.concatenate([t1 * c - t2 * s, t1 * s + t2 * c], axis=-1).astype(t.dtype)

def sliding_window_gqa(q, k, v, sinks):
    B, S, Hq, Dh = q.shape
    Hkv = k.shape[2]
    G = Hq // Hkv
    nc = S // CHUNK
    qc = q.reshape(B, nc, CHUNK, Hkv, G, Dh)

    def band(t):
        tc = t.reshape(B, nc, CHUNK, Hkv, Dh)
        shifted = [jnp.pad(tc, ((0, 0), (j, 0), (0, 0), (0, 0), (0, 0)))[:, :nc]
                   for j in range(WINDOW_CHUNKS - 1, -1, -1)]
        return jnp.concatenate(shifted, axis=2)

    kb, vb = band(k), band(v)
    scores = jnp.einsum('bcqhgd,bckhd->bchgqk', qc, kb,
                        preferred_element_type=jnp.float32) * (Dh ** -0.5)
    chunk_id = jnp.arange(nc)[:, None]
    key_offset = (WINDOW_CHUNKS - 1) - jnp.arange(WINDOW_CHUNKS * CHUNK)[None, :] // CHUNK
    valid = chunk_id >= key_offset
    scores = jnp.where(valid[None, :, None, None, None, :], scores, NEG_INF)
    sink = jnp.broadcast_to(sinks.astype(jnp.float32).reshape(1, 1, Hkv, G, 1, 1),
                            scores.shape[:-1] + (1,))
    probs = jax.nn.softmax(jnp.concatenate([scores, sink], axis=-1), axis=-1)[..., :-1]
    out = jnp.einsum('bchgqk,bckhd->bcqhgd', probs.astype(v.dtype), vb)
    return out.reshape(B, S, Hq * Dh)

def retention(q, k, v):
    B, S, H, dk = q.shape
    dv = v.shape[-1]
    nc = S // CHUNK
    log_gamma = jnp.log(1.0 - 2.0 ** (-5.0 - jnp.arange(H, dtype=jnp.float32)))
    pos = jnp.arange(CHUNK, dtype=jnp.float32)
    diff = pos[:, None] - pos[None, :]
    decay = jnp.where(diff >= 0,
                      jnp.exp(log_gamma[:, None, None] * jnp.maximum(diff, 0.0)[None]), 0.0)
    qf = q.astype(jnp.float32).reshape(B, nc, CHUNK, H, dk)
    kf = k.astype(jnp.float32).reshape(B, nc, CHUNK, H, dk) * (dk ** -0.5)
    vf = v.astype(jnp.float32).reshape(B, nc, CHUNK, H, dv)

    inner = jnp.einsum('bcnhd,bcmhd->bchnm', qf, kf) * decay[None, None]
    y_inner = jnp.einsum('bchnm,bcmhe->bcnhe', inner, vf)

    k_decay = jnp.exp(log_gamma[None, :] * (CHUNK - 1.0 - pos)[:, None])
    q_decay = jnp.exp(log_gamma[None, :] * (pos + 1.0)[:, None])
    chunk_decay = jnp.exp(log_gamma * CHUNK)

    def step(state, inp):
        qc, kc, vc = inp
        y = jnp.einsum('bnhd,bhde->bnhe', qc * q_decay[None, :, :, None], state)
        state = state * chunk_decay[None, :, None, None] + jnp.einsum(
            'bmhd,bmhe->bhde', kc * k_decay[None, :, :, None], vc)
        return state, y

    init = jnp.zeros((B, H, dk, dv), jnp.float32)
    _, y_cross = lax.scan(step, init, (jnp.swapaxes(qf, 0, 1), jnp.swapaxes(kf, 0, 1),
                                       jnp.swapaxes(vf, 0, 1)))
    y = y_inner + jnp.swapaxes(y_cross, 0, 1)
    return y.reshape(B, S, H, dv)

def peer(h, w_query, sub_keys, expert_down, expert_up):
    B, S, D = h.shape
    half = PEER_QUERY_DIM // 2
    q = (h @ w_query).reshape(B, S, PEER_HEADS, 2, half).astype(jnp.float32)
    sk = sub_keys.astype(jnp.float32)
    s1 = jnp.einsum('bshd,kd->bshk', q[..., 0, :], sk[0])
    s2 = jnp.einsum('bshd,kd->bshk', q[..., 1, :], sk[1])
    v1, i1 = lax.top_k(s1, PEER_TOPK)
    v2, i2 = lax.top_k(s2, PEER_TOPK)
    cand = (v1[..., :, None] + v2[..., None, :]).reshape(B, S, PEER_HEADS, PEER_TOPK * PEER_TOPK)
    cand_idx = (i1[..., :, None] * N_KEYS + i2[..., None, :]).reshape(B, S, PEER_HEADS, PEER_TOPK * PEER_TOPK)
    top_s, top_pos = lax.top_k(cand, PEER_TOPK)
    expert_idx = jnp.take_along_axis(cand_idx, top_pos, axis=-1)
    gates = jax.nn.softmax(top_s, axis=-1)

    n_tok = B * S
    nb = n_tok // PEER_TOKEN_BLOCK
    hk = PEER_HEADS * PEER_TOPK
    hb = h.reshape(nb, PEER_TOKEN_BLOCK, D)
    ib = expert_idx.reshape(nb, PEER_TOKEN_BLOCK, hk)
    gb = gates.reshape(nb, PEER_TOKEN_BLOCK, hk)

    def block(args):
        hx, idx, g = args
        u = jnp.take(expert_down, idx, axis=0)
        act = jax.nn.gelu(jnp.einsum('td,ted->te', hx, u, preferred_element_type=jnp.float32))
        vv = jnp.take(expert_up, idx, axis=0)
        return jnp.einsum('te,ted->td', (act * g).astype(hx.dtype), vv)

    y = lax.map(block, (hb, ib, gb))
    return y.reshape(B, S, D)

def setup_inputs(seed: int = 0) -> dict:
    key = jax.random.key(seed)
    ks = jax.random.split(key, 20)
    f32 = jnp.float32
    nrm = lambda k, shape, scale: jax.random.normal(k, shape, f32) * scale
    gain = lambda k, shape: 1.0 + 0.02 * jax.random.normal(k, shape, f32)
    return {
        "x": nrm(ks[0], (BATCH, SEQ, D_MODEL), 1.0),
        "p": nrm(ks[1], (DEPTH, BATCH, SEQ, PLE_DIM), 1.0),
        "mix_norm": gain(ks[2], (DEPTH, D_MODEL)),
        "w_in": nrm(ks[3], (DEPTH, D_MODEL, IN_W), D_MODEL ** -0.5),
        "attn_sinks": nrm(ks[4], (DEPTH, ATT_HEADS), 1.0),
        "w_o_att": nrm(ks[5], (DEPTH, ATT_Q_W, D_MODEL), ATT_Q_W ** -0.5),
        "w_o_ret": nrm(ks[6], (DEPTH, RET_V_W, D_MODEL), RET_V_W ** -0.5),
        "w_out": nrm(ks[7], (DEPTH, D_MODEL, D_MODEL), D_MODEL ** -0.5),
        "ffn_norm": gain(ks[8], (DEPTH, D_MODEL)),
        "w_peer_query": nrm(ks[9], (DEPTH, D_MODEL, PEER_HEADS * PEER_QUERY_DIM), D_MODEL ** -0.5),
        "peer_sub_keys": nrm(ks[10], (DEPTH, 2, N_KEYS, PEER_QUERY_DIM // 2), (PEER_QUERY_DIM // 2) ** -0.5),
        "peer_down": nrm(ks[11], (DEPTH, N_EXPERTS, D_MODEL), D_MODEL ** -0.5),
        "peer_up": nrm(ks[12], (DEPTH, N_EXPERTS, D_MODEL), PEER_HEADS ** -0.5),
        "ple_norm": gain(ks[13], (DEPTH, D_MODEL)),
        "w_ple_gate": nrm(ks[14], (DEPTH, D_MODEL, D_MODEL), D_MODEL ** -0.5),
        "w_ple_proj": nrm(ks[15], (DEPTH, PLE_DIM, D_MODEL), PLE_DIM ** -0.5),
        "final_norm": gain(ks[16], (D_MODEL,)),
    }

def reference(x, p, mix_norm, w_in, attn_sinks, w_o_att, w_o_ret, w_out, ffn_norm,
              w_peer_query, peer_sub_keys, peer_down, peer_up, ple_norm, w_ple_gate,
              w_ple_proj, final_norm):
    B, S, D = x.shape
    cos_a, sin_a = rope_tables(S, ATT_HEAD_DIM)
    cos_r, sin_r = rope_tables(S, RET_QK_DIM)
    split_points = [int(v) for v in np.cumsum(IN_SPLITS)[:-1]]
    for i in range(DEPTH):
        h = rms_norm(x, mix_norm[i])
        z = h @ w_in[i]
        aq, ak, av, rq, rk, rv, rg, ga, gr = jnp.split(z, split_points, axis=-1)

        aq = apply_rope(aq.reshape(B, S, ATT_HEADS, ATT_HEAD_DIM), cos_a, sin_a)
        ak = apply_rope(ak.reshape(B, S, ATT_KV_HEADS, ATT_HEAD_DIM), cos_a, sin_a)
        av = av.reshape(B, S, ATT_KV_HEADS, ATT_HEAD_DIM)
        y_att = sliding_window_gqa(aq, ak, av, attn_sinks[i]) @ w_o_att[i]

        rq = apply_rope(rq.reshape(B, S, RET_HEADS, RET_QK_DIM), cos_r, sin_r)
        rk = apply_rope(rk.reshape(B, S, RET_HEADS, RET_QK_DIM), cos_r, sin_r)
        rv = rv.reshape(B, S, RET_HEADS, RET_V_DIM)
        yr = retention(rq, rk, rv)
        mu = jnp.mean(yr, axis=-1, keepdims=True)
        var = jnp.mean(jnp.square(yr - mu), axis=-1, keepdims=True)
        yr = (yr - mu) * lax.rsqrt(var + EPS)
        yr = jax.nn.silu(rg.reshape(B, S, RET_HEADS, RET_V_DIM).astype(jnp.float32)) * yr
        y_ret = yr.reshape(B, S, RET_V_W).astype(x.dtype) @ w_o_ret[i]

        merged = jax.nn.sigmoid(ga) * y_att + jax.nn.sigmoid(gr) * y_ret
        x = x + merged @ w_out[i]

        x = x + peer(rms_norm(x, ffn_norm[i]), w_peer_query[i], peer_sub_keys[i],
                     peer_down[i], peer_up[i])

        gate = jax.nn.sigmoid(rms_norm(x, ple_norm[i]) @ w_ple_gate[i])
        x = x + gate * (p[i] @ w_ple_proj[i])
    return rms_norm(x, final_norm)


_drawn_inputs = setup_inputs


def setup_inputs(seed=0):
    import zlib

    import numpy as np

    out = dict(_drawn_inputs(seed))
    spreads = {}
    factors = {'attn_sinks': 8.0, 'ple_norm': 38.508, 'final_norm': 8.173}
    for name, (base, spread) in spreads.items():
        noise = np.random.default_rng([zlib.crc32(name.encode()), seed]).standard_normal(out[name].shape)
        drawn = base * np.exp(spread * noise) if base else spread * noise
        out[name] = __import__('jax').numpy.asarray(drawn.astype(out[name].dtype))
    for name, factor in factors.items():
        out[name] = (out[name] * factor).astype(out[name].dtype)
    return out
```

```python
from contextlib import ExitStack

import numpy as np

import concourse.bass as bass
from concourse import mybir

F32 = mybir.dt.float32
F32R = mybir.dt.float32r
BF16 = mybir.dt.bfloat16
U32 = mybir.dt.uint32
ALU = mybir.AluOpType
ACT = mybir.ActivationFunctionType
AX_X = mybir.AxisListType.X

D, S, CHUNK, EPS = 1024, 512, 64, 1e-6
AH, AKV, ADH = 8, 2, 128
RH, RDK, RDV = 4, 256, 512
PH, NKEY, TOPK = 8, 128, 16
PLE = 256
NEG = -1e30
P = 128
KT = D // P
TT = S // P
SLOTS = PH * TOPK
LOWEST = -3.0e38

AQ0, AK0, AV0 = 0, AH * ADH, AH * ADH + AKV * ADH
RQ0 = AV0 + AKV * ADH
RK0, RV0 = RQ0 + RH * RDK, RQ0 + 2 * RH * RDK
RG0 = RV0 + RH * RDV
GA0 = RG0 + RH * RDV
GR0 = GA0 + D

UW = 1024
RAW = 4
RING = 8


def weight_units():
    u = []
    for i in range(RH + 1):
        if i < RH:
            u += [("rq", 2 * i), ("rq", 2 * i + 1), ("rk", 2 * i), ("rk", 2 * i + 1)]
        if i > 0:
            u += [("wor", 4 * (i - 1) + c) for c in range(4)]
        if i < RH:
            u += [("rv", 4 * i + c) for c in range(4)] + [("rg", 4 * i + c) for c in range(4)]
    u += [("gr", m) for m in range(KT)]
    u += [("ak", 0), ("ak", 1), ("av", 0), ("av", 1)]
    u += [("aq", h) for h in range(AH)]
    for m in range(KT):
        u += [("ga", m), ("woa", m)]
    u += [("out", m) for m in range(KT)]
    u += [("pq", m) for m in range(2 * PH)]
    u += [("dn", 0), ("dn", 1)]
    for g in range(NKEY // 2):
        if g + 1 < NKEY // 2:
            u += [("dn", 2 * g + 2), ("dn", 2 * g + 3)]
        u += [("up", 2 * g), ("up", 2 * g + 1)]
    u += [("pp", 0), ("pp", 1)]
    u += [("pg", m) for m in range(KT)]
    return u


UNITS = weight_units()
NU = len(UNITS)
UNIT = {k: n for n, k in enumerate(UNITS)}
DN0 = UNIT[("dn", 0)]


def projection_outputs():
    o = []
    for i in range(RH + 1):
        if i < RH:
            o += [("rq", 2 * i), ("rq", 2 * i + 1), ("rk", 2 * i), ("rk", 2 * i + 1)]
        if i > 0:
            o += [("wor", i - 1, m) for m in range(KT)]
        if i < RH:
            o += [("rv", i, t) for t in range(TT)] + [("rg", i, t) for t in range(TT)]
    o += [("gr", m) for m in range(KT)]
    o += [("ak", 0), ("ak", 1)] + [("av", t) for t in range(TT)]
    o += [("aq", h) for h in range(AH)]
    for m in range(KT):
        o += [("ga", m), ("woa", m)]
    o += [("out", m) for m in range(KT)]
    o += [("pq", m) for m in range(2 * PH)]
    o += [("z", e) for e in range(NKEY)]
    o += [("pp", m) for m in range(KT)]
    o += [("pg", m) for m in range(KT)]
    return o


OUT = {k: n for n, k in enumerate(projection_outputs())}
LAST_UNIT = {}
for _k in OUT:
    if _k[0] in ("rv", "rg"):
        LAST_UNIT[_k] = UNIT[(_k[0], 4 * _k[1] + 3)]
    elif _k[0] == "wor":
        LAST_UNIT[_k] = UNIT[("wor", 4 * _k[1] + _k[2] // 2)]
    elif _k[0] == "av":
        LAST_UNIT[_k] = UNIT[("av", 1)]
    elif _k[0] == "z":
        LAST_UNIT[_k] = UNIT[("dn", _k[1])]
    elif _k[0] == "pp":
        LAST_UNIT[_k] = UNIT[("pp", _k[1] // 4)]
    else:
        LAST_UNIT[_k] = UNIT[_k]

S_AT = [0, 512, 896, 1152]
SMALL = 808
SCRATCH = 15104

TG = 32
NTG = S // TG
JQ = 4



def block_program(nc, xT_d, w_d, small_d, rope_r_d, decay_d, rope_a_d, mask_d, pT_d, out_d):
    gate_d = nc.dram_tensor("gate_scratch", (NTG, P, NKEY * TG), F32, kind="Internal").ap()

    with ExitStack() as ctx:
        def sb(name, shape, dt=F32):
            return ctx.enter_context(nc.sbuf_tensor(name, shape, dt))

        def sem(name):
            return ctx.enter_context(nc.semaphore(name))

        xT = sb("xT", [P, KT, S])
        raw = sb("raw", [P, RAW, UW])
        w_hi = sb("w_hi", [P, RING, UW], F32R)
        w_lo = sb("w_lo", [P, RING, UW], F32R)
        h_hi = sb("h_hi", [P, KT, S], F32R)
        h_lo = sb("h_lo", [P, KT, S], F32R)
        b_hi = sb("b_hi", [P, KT, S], F32R)
        b_lo = sb("b_lo", [P, KT, S], F32R)
        small = sb("small", [P, SMALL])
        ident, swap, ones = small[:, 0:128], small[:, 128:256], small[:, 256:384]
        iota = small[:, 384:512]
        gains = small[:, 512:544].rearrange("p (n k) -> p n k", n=4)
        sinks = small[:, 544:552]
        sub_keys = small[:, 552:808].rearrange("p (a k) -> p a k", a=2)
        misc = sb("misc", [P, 128])
        scr = sb("scr", [P, SCRATCH])

        def cut(at, n):
            assert at + n <= SCRATCH, (at, n)
            return scr[:, at:at + n]

        def cut3(at, a, b):
            return cut(at, a * b).rearrange("p (a b) -> p a b", a=a)

        yacc = cut3(0, KT, S)
        tile2 = cut3(4096, 2, S)
        prod = cut(5120, S)
        sq = cut3(8704, 2, S)
        normed = cut3(9728, 2, S)
        rrms = cut(10752, S)
        rope_r = cut3(5632, 2, S)
        decay = cut3(6656, 2, S)
        r_q = cut3(7680, 2, S)
        r_k = cut3(8704, 2, S)
        r_v = cut3(9728, TT, RDV)
        r_g = cut3(11776, TT, RDV)
        r_s = cut(13824, 1280)
        stats = misc[:, 0:24].rearrange("p (t n) -> p t n", t=TT)
        mean_var = misc[:, 24:32].rearrange("p (t n) -> p t n", t=TT)
        var_eps, std4, rstd4 = misc[:, 32:36], misc[:, 36:40], misc[:, 40:44]
        a_k = cut3(5632, AKV, S)
        a_v = cut3(6656, TT, AKV * ADH)
        a_q = cut3(7680, 2, S)
        a_s = cut(8704, 2048).rearrange("p (b t k) -> p b t k", b=2, t=TT)
        a_pT = cut(10752, 1024).rearrange("p (t b q) -> p t b q", t=TT, b=2)
        rope_a = cut3(11776, 2, S)
        mask = cut(12800, 1024).rearrange("p (t k) -> p t k", t=TT)
        smax, negmax, psum4, esink, rden = (misc[:, 48 + 4 * n:52 + 4 * n] for n in range(5))
        s12 = cut(5632, 2048).rearrange("p (m t k) -> p m t k", m=4, t=TT)
        taken = cut(7680, 256)
        cand = cut(7936, 256)
        val = cut(9216, 1024).rearrange("p (t m k) -> p t m k", t=TT, m=2 * PH)
        idx = cut(10240, 1024).bitcast(U32).rearrange("p (t m k) -> p t m k", t=TT, m=2 * PH)
        idxf = cut(11264, 1024).rearrange("p (t m k) -> p t m k", t=TT, m=2 * PH)
        top = cut(12288, 512).rearrange("p (t h k) -> p t h k", t=TT, h=PH)
        pos = cut(12800, 512).bitcast(U32).rearrange("p (t h k) -> p t h k", t=TT, h=PH)
        posu = cut(13312, 512).bitcast(U32).rearrange("p (t h k) -> p t h k", t=TT, h=PH)
        posf = cut(13824, 512).rearrange("p (t h k) -> p t h k", t=TT, h=PH)
        pick = cut(0, 2048).rearrange("p (h k j) -> p h k j", h=PH, k=TOPK)
        row_s = cut(6144, 512).rearrange("p (t n) -> p t n", t=TT)
        col_s = cut(6656, 512).rearrange("p (t n) -> p t n", t=TT)
        gate_s = cut(7168, 512).rearrange("p (t n) -> p t n", t=TT)
        gsum = misc[:, 72:104]
        stage = cut(0, 8192).rearrange("p (b j t) -> p b j t", b=2, t=TG)
        rowT, colT, g1, g2, g3 = (cut(8192 + 512 * n, S).rearrange("p (g c) -> p g c", g=NTG) for n in range(5))
        gfull = cut(10752, S)
        gpart = cut(11264, 256).bitcast(BF16)
        onehot = cut(11776, 2048).bitcast(BF16).rearrange("p (b q n k) -> p b q n k", b=2, q=4, n=4)
        iota_b = cut(13824, 64).bitcast(BF16)
        gates = cut(0, 4096).rearrange("p (b g j t) -> p b g j t", b=2, g=NTG, j=JQ)
        act = cut3(4096, 2, S)
        wgt = cut3(5120, 2, S)
        pT = cut3(14080, 2, S)
        pproj = cut3(0, KT, S)
        final = cut3(0, KT, S)

        bank = ctx.enter_context(nc.psum_tensor("bank", [P, 8, 512], F32))

        landed = [sem(f"landed{i}") for i in range(RAW)]
        hi_done = sem("hi_done")
        lo_done = sem("lo_done")
        unit_used = sem("unit_used")
        proj_done = sem("proj_done")
        proj_free = [sem("proj_free0"), sem("proj_free1")]
        x_landed, small_landed = sem("x_landed"), sem("small_landed")
        rope_r_landed, rope_a_landed, p_landed = sem("rope_r_landed"), sem("rope_a_landed"), sem("p_landed")
        decay_landed = [sem("decay_landed0"), sem("decay_landed1")]
        sq_ready, sq_used, ss_done = sem("sq_ready"), sem("sq_used"), sem("ss_done")
        ms_ready, rms_ready = sem("ms_ready"), sem("rms_ready")
        normed_ready, h_hi_ready, h_ready = sem("normed_ready"), sem("h_hi_ready"), sem("h_ready")
        x_ready = sem("x_ready")
        tile_ready, tile_free = sem("tile_ready"), sem("tile_free")
        rot_ready = sem("rot_ready")
        rs_done, rs_ready = sem("rs_done"), sem("rs_ready")
        rv_ready, rg_ready = sem("rv_ready"), sem("rg_ready")
        y_done, var_ready, std_ready, gn_done = sem("y_done"), sem("var_ready"), sem("std_ready"), sem("gn_done")
        tr_done, b_hi_ready, b_ready = sem("tr_done"), sem("b_hi_ready"), sem("b_ready")
        yacc_ready = sem("yacc_ready")
        swap_done, arot_done = sem("swap_done"), sem("arot_done")
        av_ready, sc_done, sc_read = sem("av_ready"), sem("sc_done"), sem("sc_read")
        max_ready, exp_ready, p_ready = sem("max_ready"), sem("exp_ready"), sem("p_ready")
        pt_done, pT_ready, pv_done = sem("pt_done"), sem("pT_ready"), sem("pv_done")
        ks_done, s12_ready, s12_free = sem("ks_done"), sem("s12_ready"), sem("s12_free")
        qp_ready = sem("qp_ready")
        top_ready, gexp_ready, sel_ready, selT_done = sem("top_ready"), sem("gexp_ready"), sem("sel_ready"), sem("selT_done")
        oh_ready, oh_used, stage_ready = sem("oh_ready"), sem("oh_used"), sem("stage_ready")
        gate_written = [sem("gate_written0"), sem("gate_written1")]
        gate_landed = [sem("gate_landed0"), sem("gate_landed1")]
        act_ready, wgt_ready, wgt_hi_ready, wgt_split = sem("act_ready"), sem("wgt_ready"), sem("wgt_hi_ready"), sem("wgt_split")
        up_done, up_added = sem("up_done"), sem("up_added")
        p_hi_ready, p_split, pproj_ready = sem("p_hi_ready"), sem("p_split"), sem("pproj_ready")
        final_ready, stored = sem("final_ready"), sem("stored")
        dve_step = sem("dve_step")

        block = ctx.enter_context(nc.Block())
        w_rounds = w_d[0:NU // RAW * RAW].rearrange("(r s) p n -> s r p n", s=RAW)
        gate_quads = gate_d.rearrange("g p n -> p g n")

        def proj_bank(key):
            return bank[:, OUT[key] % 2, :]

        def wait_output(eng, key):
            eng.wait_ge(proj_done, OUT[key] + 1)

        def free_of(key):
            return proj_free[OUT[key] % 2]

        @block.sync
        def _(sp):
            sp.dma_start(xT[:, :, :], xT_d).then_inc(x_landed, 16)
            sp.dma_start(small[:, :], small_d).then_inc(small_landed, 16)
            for s in range(RAW):
                sp.dma_start(raw[:, s, :], w_d[s]).then_inc(landed[s], 16)
            with sp.Fori(1, NU // RAW) as r:
                for s in range(RAW):
                    sp.wait_ge(lo_done, RAW * r + (s - RAW + 1))
                    sp.dma_start(raw[:, s, :], w_rounds[s][r]).then_inc(landed[s], 16)
            for u in range(NU // RAW * RAW, NU):
                sp.wait_ge(lo_done, u - RAW + 1)
                sp.dma_start(raw[:, u % RAW, :], w_d[u]).then_inc(landed[u % RAW], 16)
            for k in range(KT):
                sp.wait_ge(final_ready, k + 1)
                sp.dma_start(out_d[:, k, :], final[:, k, :]).then_inc(stored, 16)
            sp.wait_ge(stored, 16 * KT)

        @block.gpsimd
        def _(pool):
            def lower(s):
                return nc.gpsimd.tensor_tensor(w_lo[:, s, :], raw[:, s % RAW, :], w_hi[:, s, :].bitcast(F32),
                                               ALU.subtract)

            with pool.Fori(0, NU // RING) as r:
                for s in range(RING):
                    pool.wait_ge(hi_done, RING * r + (s + 1))
                    lower(s).then_inc(lo_done, 1)
            for u in range(NU // RING * RING, NU):
                pool.wait_ge(hi_done, u + 1)
                lower(u % RING).then_inc(lo_done, 1)

        @block.scalar
        def _(sc):
            ahead = [0]
            tiles = [0]

            def upper(u, u_mod):
                s = u_mod % RAW
                sc.wait_ge(landed[s], 4 * (u - s) + 16)
                if not isinstance(u, int) or u >= RING:
                    sc.wait_ge(unit_used, u - (RING - 1))
                nc.scalar.activation(w_hi[:, u_mod, :], raw[:, s, :], ACT.Copy).then_inc(hi_done, 1)

            def run_ahead(u):
                while ahead[0] <= min(u, NU - 1):
                    upper(ahead[0], ahead[0] % RING)
                    ahead[0] += 1

            def output(key):
                whole = key[0] in ("rv", "rg", "av")
                run_ahead(LAST_UNIT[key] + (0 if whole else 4))
                wait_output(sc, key)
                return proj_bank(key)

            def to_tile(key, func):
                src = output(key)
                z = tiles[0]
                tiles[0] += 1
                if z >= 2:
                    sc.wait_ge(tile_free, z - 1)
                ins = nc.scalar.activation(tile2[:, z % 2, :], src, func)
                ins.then_inc(tile_ready, 1)
                sc.wait_ge(tile_ready, z + 1)
                sc.sem_inc(free_of(key), 1)

            def norm(r, ready):
                for k in range(KT):
                    ready(k)
                    n = KT * r + k
                    if n >= 2:
                        sc.wait_ge(sq_used, n - 1)
                    nc.scalar.activation(sq[:, k % 2, :], xT[:, k, :], ACT.Square).then_inc(sq_ready, 1)
                sc.wait_ge(ms_ready, r + 1)
                nc.scalar.activation(rrms, rrms, ACT.Sqrt).then_inc(rms_ready, 1)

            def norm_upper(r):
                for k in range(KT):
                    sc.wait_ge(normed_ready, KT * r + k + 1)
                    nc.scalar.activation(h_hi[:, k, :], normed[:, k % 2, :], ACT.Copy).then_inc(h_hi_ready, 1)

            sc.dma_start(rope_r[:, :, :], rope_r_d).then_inc(rope_r_landed, 16)
            for i in range(2):
                sc.dma_start(decay[:, i, :], decay_d[i]).then_inc(decay_landed[i], 16)
            run_ahead(3)
            sc.wait_ge(x_landed, 16)
            sc.wait_ge(small_landed, 16)
            norm(0, lambda k: None)
            norm_upper(0)

            for i in range(RH + 1):
                if i < RH:
                    for key in (("rq", 2 * i), ("rq", 2 * i + 1), ("rk", 2 * i), ("rk", 2 * i + 1)):
                        to_tile(key, ACT.Copy)
                if i > 0:
                    for c in range(4):
                        sc.wait_ge(tr_done, 4 * (i - 1) + c + 1)
                        nc.scalar.activation(b_hi[:, c, :], bank[:, 6 + c % 2, :], ACT.Copy).then_inc(b_hi_ready, 1)
                    if 1 < i + 1 < RH:
                        sc.wait_ge(rs_ready, 4 * i)
                        sc.dma_start(decay[:, (i + 1) % 2, :], decay_d[i + 1]).then_inc(decay_landed[(i + 1) % 2], 16)
                if i < RH:
                    for t in range(TT):
                        src = output(("rv", i, t))
                        if i > 0 and t == 0:
                            sc.wait_ge(y_done, TT * i)
                        nc.scalar.activation(r_v[:, t, :], src, ACT.Copy).then_inc(rv_ready, 1)
                        sc.wait_ge(rv_ready, TT * i + t + 1)
                        sc.sem_inc(free_of(("rv", i, t)), 1)
                    for t in range(TT):
                        src = output(("rg", i, t))
                        nc.scalar.activation(r_g[:, t, :], src, ACT.Silu).then_inc(rg_ready, 1)
                        sc.wait_ge(rg_ready, TT * i + t + 1)
                        sc.sem_inc(free_of(("rg", i, t)), 1)
                    sc.wait_ge(var_ready, i + 1)
                    nc.scalar.activation(std4, var_eps, ACT.Sqrt).then_inc(std_ready, 1)
            sc.wait_ge(tr_done, 4 * RH)
            sc.dma_start(rope_a[:, :, :], rope_a_d).then_inc(rope_a_landed, 16)
            sc.dma_start(mask, mask_d).then_inc(rope_a_landed, 16)
            for m in range(KT):
                to_tile(("gr", m), ACT.Sigmoid)

            to_tile(("ak", 0), ACT.Copy)
            to_tile(("ak", 1), ACT.Copy)
            for t in range(TT):
                src = output(("av", t))
                nc.scalar.activation(a_v[:, t, :], src[:, 0:AKV * ADH], ACT.Copy).then_inc(av_ready, 1)
                sc.wait_ge(av_ready, t + 1)
                sc.sem_inc(free_of(("av", t)), 1)
            for i in range(AH + 4):
                if i < AH:
                    to_tile(("aq", i), ACT.Copy)
                if 0 <= i - 2 < AH:
                    h = i - 2
                    sc.wait_ge(max_ready, h + 1)
                    for t in range(TT):
                        nc.scalar.activation(a_s[:, h % 2, t, :], a_s[:, h % 2, t, :], ACT.Exp,
                                             bias=negmax[:, t:t + 1], accum_out=psum4[:, t:t + 1])
                    nc.scalar.activation(esink, negmax, ACT.Exp, bias=sinks[:, h:h + 1]).then_inc(exp_ready, 1)
                if 0 <= i - 3 < AH:
                    h = i - 3
                    sc.wait_ge(pt_done, h + 1)
                    if h > 0:
                        sc.wait_ge(pv_done, h)
                    nc.scalar.activation(a_pT.rearrange("p t b q -> p (t b q)"),
                                         bank[:, 5:7, :].rearrange("p a b -> p (a b)"), ACT.Copy).then_inc(pT_ready, 1)
                if 0 <= i - 4 < AH:
                    h = i - 4
                    sc.wait_ge(pv_done, h + 1)
                    nc.scalar.activation(b_hi[:, h, :], bank[:, 7, :], ACT.Copy).then_inc(b_hi_ready, 1)
            for m in range(KT):
                to_tile(("ga", m), ACT.Sigmoid)
            run_ahead(UNIT[("woa", KT - 1)] + 4)
            wait_output(sc, ("woa", KT - 1))
            for m in range(KT):
                sc.wait_ge(yacc_ready, RH * KT + m + 1)
                nc.scalar.activation(h_hi[:, m, :], yacc[:, m, :], ACT.Copy).then_inc(h_hi_ready, 1)
            run_ahead(UNIT[("out", KT - 1)])
            norm(1, lambda k: sc.wait_ge(x_ready, k + 1))
            for k in range(KT):
                sc.wait_ge(normed_ready, KT + k + 1)
                nc.scalar.activation(h_hi[:, k, :], normed[:, k % 2, :], ACT.Copy).then_inc(h_hi_ready, 1)

            def key_scores(m):
                sc.wait_ge(ks_done, m + 1)
                if m >= 4:
                    sc.wait_ge(s12_free, m - 3)
                nc.scalar.activation(s12[:, m % 4].rearrange("p t k -> p (t k)"), bank[:, 2 + m % 2, :],
                                     ACT.Copy).then_inc(s12_ready, 1)

            for m in range(2 * PH):
                src = output(("pq", m))
                if m >= 2:
                    sc.wait_ge(ks_done, m - 1)
                nc.scalar.activation(tile2[:, m % 2, :], src, ACT.Copy).then_inc(qp_ready, 1)
                sc.wait_ge(qp_ready, m + 1)
                sc.sem_inc(free_of(("pq", m)), 1)
                if m > 0:
                    key_scores(m - 1)
            key_scores(2 * PH - 1)
            sc.wait_ge(top_ready, 1)
            nc.scalar.activation(gate_s.rearrange("p t n -> p (t n)"), gate_s.rearrange("p t n -> p (t n)"),
                                 ACT.Exp).then_inc(gexp_ready, 1)

            run_ahead(DN0 + 5)

            def move_gates(it):
                for b in range(2):
                    if not isinstance(it, int):
                        sc.wait_ge(gate_written[b], 16 * it)
                    for q in range(TG // 4):
                        n = 16 * it + (8 * b + q)
                        sc.wait_ge(oh_used, n + 1)
                        nc.scalar.activation(stage[:, b, :, 4 * q:4 * q + 4].rearrange("p j t -> p t j"),
                                             bank[:, 2 + q % 4, :].rearrange("p (t j) -> p t j", t=4),
                                             ACT.Copy).then_inc(stage_ready, 1)
                    sc.wait_ge(stage_ready, 16 * it + (8 * b + 8))
                    sc.dma_start(gate_pairs[b][it], stage[:, b].rearrange("p j t -> p (j t)")).then_inc(gate_written[b], 16)

            gate_pairs = gate_d.rearrange("(i b) p n -> b i p n", b=2)
            move_gates(0)
            with sc.Fori(1, NTG // 2) as it:
                move_gates(it)
            for b in range(2):
                sc.wait_ge(gate_written[b], 16 * (NTG // 2))

            def read_gates(quad, b):
                nc.scalar.dma_start(gates[:, b].rearrange("p g j t -> p g (j t)"), quad).then_inc(gate_landed[b], 16)

            def gate_src(q):
                return gate_quads[:, :, q * JQ * TG:(q + 1) * JQ * TG]

            quads2 = gate_d.rearrange("g p (i b n) -> b i p g n", b=2, n=JQ * TG)

            def gelu(e, e8):
                sc.wait_ge(proj_done, e + (OUT[("z", 0)] + 1))
                if not isinstance(e, int) or e >= 2:
                    sc.wait_ge(wgt_ready, e - 1)
                nc.scalar.activation(act[:, e8 % 2, :], bank[:, (OUT[("z", 0)] + e8) % 2, :],
                                     ACT.Gelu_apprx_tanh).then_inc(act_ready, 1)

            def gelu_free(e, e8):
                sc.wait_ge(act_ready, e + 1)
                sc.sem_inc(proj_free[(OUT[("z", 0)] + e8) % 2], 1)

            def weight_upper(e, e8):
                sc.wait_ge(wgt_ready, e + 1)
                if not isinstance(e, int) or e >= 4:
                    sc.wait_ge(up_done, 4 * (e - e8 % 2) - 8)
                nc.scalar.activation(b_hi[:, e8 % 4, :], wgt[:, e8 % 2, :], ACT.Copy).then_inc(wgt_hi_ready, 1)

            nc.scalar.dma_start(gates[:, 0].rearrange("p g j t -> p g (j t)"), quads2[0][0]).then_inc(gate_landed[0], 16)
            nc.scalar.dma_start(pT[:, :, :], pT_d).then_inc(p_landed, 16)
            for e in range(2):
                gelu(e, e)
                gelu_free(e, e)
                weight_upper(e, e)
            sc.wait_ge(p_landed, 16)
            for k in range(2):
                nc.scalar.activation(b_hi[:, 4 + k, :], pT[:, k, :], ACT.Copy).then_inc(p_hi_ready, 1)
            assert ahead[0] == DN0 + 6

            def expert_step(it, last=False):
                for gg in range(4):
                    final_group = last and gg == 3
                    for c in range(2):
                        e8 = 2 * gg + 2 + c
                        e = 8 * it + e8
                        if final_group:
                            continue
                        few = last and gg == 2
                        for n in ((c,) if few else (2 * c, 2 * c + 1)):
                            n += DN0 + 4 * gg + 6
                            upper(16 * it + n, n % RING)
                        gelu(e, e8)
                        gelu_free(e, e8)
                        if c == 0 and e8 % 4 == 2 and not (last and e8 == 6):
                            b = (e8 // 4 + 1) % 2
                            nxt = 2 * it + (e8 // 4 + 1)
                            if not (isinstance(it, int) and it == 0 and e8 == 2):
                                sc.wait_ge(wgt_ready, 8 * it + (e8 - 2))
                            src = quads2[b][it] if e8 == 2 else quads2[b][it + 1]
                            nc.scalar.dma_start(gates[:, b].rearrange("p g j t -> p g (j t)"),
                                                src).then_inc(gate_landed[b], 16)
                        weight_upper(e, e8)

            expert_step(0)
            with sc.Fori(1, NKEY // 8 - 1) as it:
                expert_step(it)
            expert_step(NKEY // 8 - 1, last=True)
            ahead[0] = UNIT[("up", NKEY - 1)] + 1

            for m in range(KT):
                src = output(("pp", m))
                if m == 0:
                    sc.wait_ge(wgt_ready, NKEY)
                nc.scalar.activation(pproj[:, m, :], src, ACT.Copy).then_inc(pproj_ready, 1)
                sc.wait_ge(pproj_ready, m + 1)
                sc.sem_inc(free_of(("pp", m)), 1)
            norm(2, lambda k: sc.wait_ge(up_added, KT * (NKEY // 2 - 1) + k + 1))
            for k in range(KT):
                sc.wait_ge(normed_ready, 2 * KT + k + 1)
                nc.scalar.activation(h_hi[:, k, :], normed[:, k % 2, :], ACT.Copy).then_inc(h_hi_ready, 1)
            for m in range(KT):
                to_tile(("pg", m), ACT.Sigmoid)
            norm(3, lambda k: sc.wait_ge(x_ready, KT + k + 1))

        @block.tensor
        def _(pe):
            def mm3(out, a_hi, a_lo, c_hi, c_lo, first, last):
                nc.tensor.matmul(out, a_hi, c_hi, start=first, stop=False)
                nc.tensor.matmul(out, a_hi, c_lo, start=False, stop=False)
                return nc.tensor.matmul(out, a_lo, c_hi, start=False, stop=last)

            def bank_free(key):
                n = OUT[key]
                if n >= 2:
                    pe.wait_ge(proj_free[n % 2], n // 2)

            def columns(key, r_hi, r_lo, kt=KT, u=None, at=0, width=P, last_use=True):
                u = UNIT[key] if u is None else u
                pe.wait_ge(lo_done, u + 1)
                bank_free(key)
                s = u % RING
                for k in range(kt):
                    o = k * width + at
                    ins = mm3(proj_bank(key), w_hi[:, s, o:o + P], w_lo[:, s, o:o + P],
                              r_hi[:, k, :], r_lo[:, k, :], k == 0, k == kt - 1)
                ins.then_inc(proj_done, 1)
                if last_use:
                    pe.wait_ge(proj_done, OUT[key] + 1)
                    pe.sem_inc(unit_used, 1)

            def tokens(keys, kind, u0, nu):
                pe.wait_ge(lo_done, u0 + nu)
                s = u0 % RING
                assert s + nu <= RING
                for t, key in enumerate(keys):
                    bank_free(key)
                    o = proj_bank(key)[:, 0:nu * P]
                    for k in range(KT):
                        ins = mm3(o, h_hi[:, k, P * t:P * t + P], h_lo[:, k, P * t:P * t + P],
                                  w_hi[:, s:s + nu, k * P:k * P + P], w_lo[:, s:s + nu, k * P:k * P + P],
                                  k == 0, k == KT - 1)
                    ins.then_inc(proj_done, 1)
                pe.wait_ge(proj_done, OUT[keys[-1]] + 1)
                pe.sem_inc(unit_used, nu)

            def norm(r):
                for k in range(KT):
                    pe.wait_ge(sq_ready, KT * r + k + 1)
                    ins = nc.tensor.matmul(bank[:, 7, :], ones, sq[:, k % 2, :], start=k == 0, stop=k == KT - 1)
                    ins.then_inc(sq_used, 1)

            pe.wait_ge(small_landed, 16)
            norm(0)
            pe.wait_ge(h_ready, KT)
            for i in range(RH + 1):
                if i < RH:
                    for key in (("rq", 2 * i), ("rq", 2 * i + 1), ("rk", 2 * i), ("rk", 2 * i + 1)):
                        columns(key, h_hi, h_lo)
                if i > 0:
                    pe.wait_ge(gn_done, TT * i)
                    for c in range(4):
                        n = 4 * (i - 1) + c
                        if n >= 2:
                            pe.wait_ge(b_ready, n - 1)
                        for t in range(TT):
                            ins = nc.tensor.transpose(bank[:, 6 + c % 2, P * t:P * t + P],
                                                      r_g[:, t, P * c:P * c + P], ident)
                        ins.then_inc(tr_done, 1)
                    pe.wait_ge(b_ready, 4 * i)
                    for m in range(KT):
                        columns(("wor", i - 1, m), b_hi, b_lo, kt=4, u=UNIT[("wor", 4 * (i - 1) + m // 2)],
                                at=P * (m % 2), width=2 * P, last_use=m % 2 == 1)
                if i < RH:
                    tokens([("rv", i, t) for t in range(TT)], "rv", UNIT[("rv", 4 * i)], 4)
                    pe.wait_ge(rot_ready, 2 * i + 2)
                    if i > 0:
                        pe.wait_ge(gn_done, TT * i)
                    for j in range(TT):
                        for c in range(2):
                            ins = nc.tensor.matmul(bank[:, 2 + j, 0:S - P * j], r_k[:, c, P * j:P * j + P],
                                                   r_q[:, c, P * j:S], start=c == 0, stop=c == 1)
                        ins.then_inc(rs_done, 1)
                    tokens([("rg", i, t) for t in range(TT)], "rg", UNIT[("rg", 4 * i)], 4)
                    pe.wait_ge(rs_ready, TT * (i + 1))
                    pe.wait_ge(rv_ready, TT * (i + 1))
                    for t in range(TT):
                        for j in range(t + 1):
                            o = S_AT[j] + P * (t - j)
                            ins = nc.tensor.matmul(bank[:, 2 + t, :], r_s[:, o:o + P], r_v[:, j, :],
                                                   start=j == 0, stop=j == t)
                        ins.then_inc(y_done, 1)
            for m in range(KT):
                columns(("gr", m), h_hi, h_lo)

            def swap_halves(r, z):
                pe.wait_ge(tile_ready, z + 1)
                if r > 0:
                    pe.wait_ge(arot_done, r)
                nc.tensor.matmul(bank[:, 2, :], swap, tile2[:, z % 2, :], start=True, stop=True).then_inc(swap_done, 1)

            z0 = 4 * RH + KT
            columns(("ak", 0), h_hi, h_lo)
            columns(("ak", 1), h_hi, h_lo)
            swap_halves(0, z0)
            tokens([("av", t) for t in range(TT)], "av", UNIT[("av", 0)], 2)
            swap_halves(1, z0 + 1)
            for i in range(AH + 4):
                if i < AH:
                    columns(("aq", i), h_hi, h_lo)
                if 1 <= i <= AH:
                    swap_halves(i + 1, z0 + i + 1)
                if 0 <= i - 2 < AH:
                    h = i - 2
                    kv = h // (AH // AKV)
                    pe.wait_ge(arot_done, h + 3)
                    if h > 0:
                        pe.wait_ge(sc_read, h)
                    for t in range(TT):
                        o = bank[:, 3 + t // 2, 256 * (t % 2):256 * (t % 2) + 256]
                        q = a_q[:, h % 2, P * t:P * t + P]
                        if t == 0:
                            nc.tensor.matmul(o[:, 0:P], q, a_k[:, kv, 0:P], start=True, stop=True)
                            nc.tensor.matmul(o[:, P:2 * P], q, a_k[:, kv, 0:P], start=True, stop=True)
                        else:
                            ins = nc.tensor.matmul(o, q, a_k[:, kv, P * (t - 1):P * (t + 1)], start=True, stop=True)
                    ins.then_inc(sc_done, 1)
                if 0 <= i - 3 < AH:
                    h = i - 3
                    pe.wait_ge(p_ready, h + 1)
                    if h > 0:
                        pe.wait_ge(pT_ready, h)
                    for t in range(TT):
                        for b in range(2):
                            o = ((t % 2) * 2 + b) * P
                            ins = nc.tensor.transpose(bank[:, 5 + t // 2, o:o + P],
                                                      a_s[:, h % 2, t, P * b:P * b + P], ident)
                    ins.then_inc(pt_done, 1)
                if 0 <= i - 4 < AH:
                    h = i - 4
                    kv = h // (AH // AKV)
                    pe.wait_ge(pT_ready, h + 1)
                    pe.wait_ge(av_ready, TT)
                    if h > 0:
                        pe.wait_ge(b_ready, 4 * RH + h)
                    for t in range(TT):
                        for b in range(2):
                            if t == 0 and b == 0:
                                continue
                            ins = nc.tensor.matmul(bank[:, 7, P * t:P * t + P], a_v[:, t - 1 + b, P * kv:P * kv + P],
                                                   a_pT[:, t, b, :], start=b == 0 or t == 0, stop=b == 1)
                    ins.then_inc(pv_done, 1)
            for m in range(KT):
                columns(("ga", m), h_hi, h_lo)
                if m == 0:
                    pe.wait_ge(b_ready, 4 * RH + AH)
                columns(("woa", m), b_hi, b_lo)
            pe.wait_ge(h_ready, 2 * KT)
            for m in range(KT):
                columns(("out", m), h_hi, h_lo)
            norm(1)
            pe.wait_ge(h_ready, 3 * KT)

            def key_scores(m):
                pe.wait_ge(qp_ready, m + 1)
                if m >= 2:
                    pe.wait_ge(s12_ready, m - 1)
                for t in range(TT):
                    ins = nc.tensor.matmul(bank[:, 2 + m % 2, P * t:P * t + P], tile2[:, m % 2, P * t:P * t + P],
                                           sub_keys[:, m % 2, :], start=True, stop=True)
                ins.then_inc(ks_done, 1)

            for m in range(2 * PH):
                columns(("pq", m), h_hi, h_lo)
                if m > 0:
                    key_scores(m - 1)
            key_scores(2 * PH - 1)

            pe.wait_ge(s12_ready, 2 * PH)
            pe.wait_ge(sel_ready, 1)
            for n, src in enumerate((row_s, col_s, gate_s)):
                for t in range(TT):
                    ins = nc.tensor.transpose(bank[:, 4 + n, P * t:P * t + P], src[:, t, :], ident)
            ins.then_inc(selT_done, 1)

            def scatter(it, peeled=False):
                for b in range(2):
                    for q in range(TG // 4):
                        n = 16 * it + (8 * b + q)
                        pe.wait_ge(oh_ready, n + 1)
                        if not (peeled and 8 * b + q < 4):
                            pe.wait_ge(stage_ready, n - 3)
                        for x in range(4):
                            for part in range(3):
                                ins = nc.tensor.matmul(bank[:, 2 + q % 4, P * x:P * x + P], onehot[:, q % 2, x, 0, :],
                                                       onehot[:, q % 2, x, 1 + part, :], start=part == 0, stop=part == 2)
                        ins.then_inc(oh_used, 1)

            scatter(0, peeled=True)
            with pe.Fori(1, NTG // 2) as it:
                scatter(it)
            pe.wait_ge(stage_ready, S // 4)

            def down_step(it, e8):
                u_c = DN0 + (e8 if e8 < 2 else 2 + 4 * ((e8 - 2) // 2) + e8 % 2)
                pe.wait_ge(lo_done, 16 * it + (u_c + 1))
                n_c = OUT[("z", 0)] + e8
                pe.wait_ge(proj_free[n_c % 2], 4 * it + n_c // 2)
                s = u_c % RING
                for k in range(KT):
                    ins = mm3(bank[:, n_c % 2, :], w_hi[:, s, P * k:P * k + P], w_lo[:, s, P * k:P * k + P],
                              h_hi[:, k, :], h_lo[:, k, :], k == 0, k == KT - 1)
                ins.then_inc(proj_done, 1)
                pe.wait_ge(proj_done, 8 * it + (n_c + 1))
                pe.sem_inc(unit_used, 1)

            def up_step(it, gg, last_group=False):
                u_c = DN0 + 4 * gg + (2 if last_group else 4)
                pe.wait_ge(lo_done, 16 * it + (u_c + 2))
                pe.wait_ge(wgt_split, 8 * it + (2 * gg + 2))
                for m in range(KT):
                    if not (isinstance(it, int) and 32 * it + KT * gg + m < 4):
                        pe.wait_ge(up_added, 32 * it + (KT * gg + m - 3))
                    for c in range(2):
                        s = (u_c + c) % RING
                        w = (2 * gg + c) % 4
                        ins = mm3(bank[:, 2 + m % 4, :], w_hi[:, s, P * m:P * m + P], w_lo[:, s, P * m:P * m + P],
                                  b_hi[:, w, :], b_lo[:, w, :], c == 0, c == 1)
                    ins.then_inc(up_done, 1)
                pe.wait_ge(up_done, 32 * it + KT * (gg + 1))
                pe.sem_inc(unit_used, 2)

            def expert_step(it, last=False):
                for gg in range(4):
                    last_group = last and gg == 3
                    if not last_group:
                        down_step(it, 2 * gg + 2)
                        down_step(it, 2 * gg + 3)
                    up_step(it, gg, last_group)

            down_step(0, 0)
            down_step(0, 1)
            expert_step(0)
            with pe.Fori(1, NKEY // 8 - 1) as it:
                expert_step(it)
            expert_step(NKEY // 8 - 1, last=True)

            pe.wait_ge(p_split, 2)
            for m in range(KT):
                columns(("pp", m), b_hi[:, 4:6], b_lo[:, 4:6], kt=2, u=UNIT[("pp", m // 4)], at=P * (m % 4),
                        width=4 * P, last_use=m % 4 == 3)
            norm(2)
            pe.wait_ge(h_ready, 4 * KT)
            for m in range(KT):
                columns(("pg", m), h_hi, h_lo)
            norm(3)

        @block.vector
        def _(ve):
            steps = [0]
            tiles = [0]

            def step(ins):
                steps[0] += 1
                ins.then_inc(dve_step, 1)
                ve.wait_ge(dve_step, steps[0])

            counts = {}

            def mark(ins, signal):
                counts[signal.name] = counts.get(signal.name, 0) + 1
                ins.then_inc(signal, 1)
                ve.wait_ge(signal, counts[signal.name])

            tt, ts, stt = nc.vector.tensor_tensor, nc.vector.tensor_scalar, nc.vector.scalar_tensor_tensor

            def norm_scale(r):
                ve.wait_ge(sq_used, KT * (r + 1))
                mark(ts(rrms, bank[:, 7, :], 1.0 / D, EPS, ALU.mult, ALU.add), ms_ready)
                ve.wait_ge(rms_ready, r + 1)
                step(nc.vector.reciprocal(rrms, rrms))

            def norm(r):
                norm_scale(r)
                hb = {0: 0, 1: 2 * KT, 2: 3 * KT}[r]
                for k in range(KT):
                    mark(stt(out=normed[:, k % 2, :], in0=xT[:, k, :], scalar=gains[:, r, k:k + 1], in1=rrms,
                        op0=ALU.mult, op1=ALU.mult), normed_ready)
                    ve.wait_ge(h_hi_ready, hb + k + 1)
                    mark(tt(h_lo[:, k, :], normed[:, k % 2, :], h_hi[:, k, :].bitcast(F32), ALU.subtract), h_ready)

            def next_tile():
                z = tiles[0]
                tiles[0] += 1
                ve.wait_ge(tile_ready, z + 1)
                return tile2[:, z % 2, :]

            ve.wait_ge(x_landed, 16)
            ve.wait_ge(small_landed, 16)
            norm(0)

            def rotate_pair(dst):
                z1, z2 = next_tile(), next_tile()
                c, s = rope_r[:, 0, :], rope_r[:, 1, :]
                step(tt(dst[:, 0, :], z1, c, ALU.mult))
                step(tt(prod, z2, s, ALU.mult))
                step(tt(dst[:, 0, :], dst[:, 0, :], prod, ALU.subtract))
                mark(tt(prod, z1, s, ALU.mult), tile_free)
                step(tt(dst[:, 1, :], z2, c, ALU.mult))
                ve.sem_inc(tile_free, 1)
                mark(tt(dst[:, 1, :], dst[:, 1, :], prod, ALU.add), rot_ready)

            ve.wait_ge(rope_r_landed, 16)
            for i in range(RH + 1):
                if i < RH:
                    if i > 0:
                        ve.wait_ge(rs_done, TT * i)
                    rotate_pair(r_q)
                    rotate_pair(r_k)
                if i > 0:
                    for c in range(4):
                        n = 4 * (i - 1) + c
                        ve.wait_ge(b_hi_ready, n + 1)
                        mark(tt(b_lo[:, c, :], bank[:, 6 + c % 2, :], b_hi[:, c, :].bitcast(F32),
                           ALU.subtract), b_ready)
                    for m in range(KT):
                        key = ("wor", i - 1, m)
                        wait_output(ve, key)
                        if i == 1:
                            ins = nc.vector.tensor_copy(yacc[:, m, :], proj_bank(key))
                        else:
                            ins = tt(yacc[:, m, :], proj_bank(key), yacc[:, m, :], ALU.add)
                        mark(ins, yacc_ready)
                        ve.sem_inc(free_of(key), 1)
                if i < RH:
                    ve.wait_ge(decay_landed[i % 2], 16 * (i // 2 + 1))
                    if i > 0:
                        ve.wait_ge(y_done, TT * i)
                    for j in range(TT):
                        ve.wait_ge(rs_done, TT * i + j + 1)
                        n = S - P * j
                        mark(tt(r_s[:, S_AT[j]:S_AT[j] + n], bank[:, 2 + j, 0:n], decay[:, i % 2, 0:n],
                           ALU.mult), rs_ready)
                    for t in range(TT):
                        ve.wait_ge(y_done, TT * i + t + 1)
                        step(nc.vector.bn_stats(stats[:, t, :], bank[:, 2 + t, :]))
                        step(nc.vector.bn_aggr(mean_var[:, t, :], stats[:, t, :]))
                    mark(ts(var_eps, mean_var[:, :, 1], EPS, None, ALU.add), var_ready)
                    ve.wait_ge(std_ready, i + 1)
                    step(nc.vector.reciprocal(rstd4, std4))
                    ve.wait_ge(rg_ready, TT * (i + 1))
                    for t in range(TT):
                        step(stt(out=r_g[:, t, :], in0=bank[:, 2 + t, :], scalar=mean_var[:, t, 0:1],
                                 in1=r_g[:, t, :], op0=ALU.subtract, op1=ALU.mult))
                        mark(ts(r_g[:, t, :], r_g[:, t, :], rstd4[:, t:t + 1], None, ALU.mult), gn_done)
            for m in range(KT):
                z = next_tile()
                mark(tt(yacc[:, m, :], yacc[:, m, :], z, ALU.mult), tile_free)

            ve.wait_ge(rope_a_landed, 32)

            def rotate(r, dst):
                z = next_tile()
                ve.wait_ge(swap_done, r + 1)
                step(tt(prod, bank[:, 2, :], rope_a[:, 1, :], ALU.mult))
                step(tt(dst, z, rope_a[:, 0, :], ALU.mult))
                step(tt(dst, dst, prod, ALU.add))
                ve.sem_inc(tile_free, 1)
                ve.sem_inc(arot_done, 1)

            rotate(0, a_k[:, 0, :])
            rotate(1, a_k[:, 1, :])
            for i in range(1, AH + 4):
                if i <= AH:
                    h = i - 1
                    if h >= 2:
                        ve.wait_ge(sc_done, h - 1)
                    rotate(h + 2, a_q[:, h % 2, :])
                if 0 <= i - 2 < AH:
                    h = i - 2
                    ve.wait_ge(sc_done, h + 1)
                    if h >= 2:
                        ve.wait_ge(pt_done, h - 1)
                    step(stt(out=a_s[:, h % 2].rearrange("p t k -> p (t k)"),
                             in0=bank[:, 3:5, :].rearrange("p a b -> p (a b)"), scalar=float(ADH) ** -0.5,
                             in1=mask.rearrange("p t k -> p (t k)"), op0=ALU.mult, op1=ALU.add))
                    ve.sem_inc(sc_read, 1)
                    step(nc.vector.tensor_reduce(smax, a_s[:, h % 2], AX_X, ALU.max))
                    step(ts(smax, smax, sinks[:, h:h + 1], None, ALU.max))
                    mark(ts(negmax, smax, -1.0, None, ALU.mult), max_ready)
                    ve.wait_ge(exp_ready, h + 1)
                    step(tt(rden, psum4, esink, ALU.add))
                    step(nc.vector.reciprocal(rden, rden))
                    for t in range(TT):
                        step(ts(a_s[:, h % 2, t, :], a_s[:, h % 2, t, :], rden[:, t:t + 1], None, ALU.mult))
                    ve.sem_inc(p_ready, 1)
                if 0 <= i - 4 < AH:
                    h = i - 4
                    ve.wait_ge(b_hi_ready, 4 * RH + h + 1)
                    mark(tt(b_lo[:, h, :], bank[:, 7, :], b_hi[:, h, :].bitcast(F32), ALU.subtract), b_ready)
            for m in range(KT):
                z = next_tile()
                key = ("woa", m)
                wait_output(ve, key)
                step(tt(prod, proj_bank(key), z, ALU.mult))
                ve.sem_inc(tile_free, 1)
                ve.sem_inc(free_of(key), 1)
                mark(tt(yacc[:, m, :], yacc[:, m, :], prod, ALU.add), yacc_ready)
            for m in range(KT):
                ve.wait_ge(h_hi_ready, KT + m + 1)
                mark(tt(h_lo[:, m, :], yacc[:, m, :], h_hi[:, m, :].bitcast(F32), ALU.subtract), h_ready)
            for m in range(KT):
                key = ("out", m)
                wait_output(ve, key)
                mark(tt(xT[:, m, :], proj_bank(key), xT[:, m, :], ALU.add), x_ready)
                ve.sem_inc(free_of(key), 1)
            norm(1)

            def best(src, values, places):
                step(nc.vector.max(values[:, 0:8], src))
                step(nc.vector.max_index(places[:, 0:8], values[:, 0:8], src))
                rest = taken[:, 0:src.shape[-1]]
                step(nc.vector.match_replace(rest, values[:, 0:8], src, LOWEST))
                step(nc.vector.max(values[:, 8:16], rest))
                return nc.vector.max_index(places[:, 8:16], values[:, 8:16], rest)

            for m in range(2 * PH):
                ve.wait_ge(s12_ready, m + 1)
                for t in range(TT):
                    step(best(s12[:, m % 4, t, :], val[:, t, m, :], idx[:, t, m, :]))
                ve.sem_inc(s12_free, 1)
                if m % 2 == 1:
                    h = m // 2
                    for t in range(TT):
                        step(tt(cand.rearrange("p (a b) -> p a b", a=TOPK),
                                val[:, t, m - 1, :].unsqueeze(2).to_broadcast([P, TOPK, TOPK]),
                                val[:, t, m, :].unsqueeze(1).to_broadcast([P, TOPK, TOPK]), ALU.add))
                        step(best(cand, top[:, t, h, :], pos[:, t, h, :]))
            g4 = gate_s.rearrange("p t (h k) -> p (t h) k", h=PH)
            top3 = top.rearrange("p t h k -> p (t h) k")
            ve.wait_ge(s12_ready, 2 * PH)
            mark(tt(g4, top3, top3[:, :, 0:1].to_broadcast([P, TT * PH, TOPK]), ALU.subtract), top_ready)
            step(nc.vector.tensor_copy(idxf, idx))
            ve.wait_ge(gexp_ready, 1)
            step(nc.vector.tensor_reduce(gsum, g4, AX_X, ALU.add))
            step(nc.vector.reciprocal(gsum, gsum))
            step(tt(g4, g4, gsum.unsqueeze(2).to_broadcast([P, TT * PH, TOPK]), ALU.mult))
            for half, dst in ((0, row_s), (1, col_s)):
                if half == 0:
                    step(ts(posu, pos, 4, None, ALU.logical_shift_right))
                else:
                    step(ts(posu, pos, TOPK - 1, None, ALU.bitwise_and))
                step(nc.vector.tensor_copy(posf, posu))
                for t in range(TT):
                    step(tt(pick, posf[:, t].unsqueeze(3).to_broadcast([P, PH, TOPK, TOPK]),
                            iota[:, 0:TOPK].unsqueeze(1).unsqueeze(1).to_broadcast([P, PH, TOPK, TOPK]), ALU.is_equal))
                    step(tt(pick, pick, idxf[:, t, half::2, :].unsqueeze(2).to_broadcast([P, PH, TOPK, TOPK]), ALU.mult))
                    step(nc.vector.tensor_reduce(dst[:, t].rearrange("p (h k) -> p h k", h=PH), pick, AX_X, ALU.add))
            ve.sem_inc(sel_ready, 1)
            ve.wait_ge(selT_done, 1)

            def flat(x):
                return x.rearrange("p g c -> p (g c)")

            step(nc.vector.tensor_copy(flat(rowT), bank[:, 4, :]))
            step(nc.vector.tensor_copy(flat(colT), bank[:, 5, :]))
            step(nc.vector.tensor_copy(gfull, bank[:, 6, :]))
            step(nc.vector.tensor_copy(iota_b, iota))
            for part in (g1, g2, g3):
                step(nc.vector.tensor_copy(gpart, gfull))
                step(nc.vector.tensor_copy(flat(part), gpart))
                step(tt(gfull, gfull, flat(part), ALU.subtract))

            def one_hots(it, peeled=False):
                for b in range(2):
                    for q in range(TG // 4):
                        n = 16 * it + (8 * b + q)
                        if not (peeled and 8 * b + q < 2):
                            ve.wait_ge(oh_used, n - 1)
                        for x in range(4):
                            c = 4 * q + x
                            row, col = rowT2[:, b, it, c:c + 1], colT2[:, b, it, c:c + 1]
                            ts(onehot[:, q % 2, x, 0, :], iota_b, row, None, ALU.is_equal)
                            for k, part in enumerate(parts2):
                                ins = ts(onehot[:, q % 2, x, 1 + k, :], iota_b, col, part[:, b, it, c:c + 1],
                                         ALU.is_equal, ALU.mult)
                        ins.then_inc(oh_ready, 1)

            def by_pair(x):
                return x.rearrange("p (i b) c -> p b i c", b=2)

            rowT2, colT2, parts2 = by_pair(rowT), by_pair(colT), [by_pair(g) for g in (g1, g2, g3)]
            one_hots(0, peeled=True)
            with ve.Fori(1, NTG // 2) as it:
                one_hots(it)

            def weigh(it, e8, q_par, q_count):
                ve.wait_ge(act_ready, 8 * it + (e8 + 1))
                ve.wait_ge(gate_landed[q_par], 16 * it + 16 * q_count)
                tt(wgt[:, e8 % 2, :].rearrange("p (g t) -> p g t", g=NTG),
                   act[:, e8 % 2, :].rearrange("p (g t) -> p g t", g=NTG),
                   gates[:, q_par, :, e8 % 4, :], ALU.mult).then_inc(wgt_ready, 1)
                ve.wait_ge(wgt_hi_ready, 8 * it + (e8 + 1))
                tt(b_lo[:, e8 % 4, :], wgt[:, e8 % 2, :], b_hi[:, e8 % 4, :].bitcast(F32),
                   ALU.subtract).then_inc(wgt_split, 1)

            def add_up(it, gg):
                for m in range(KT):
                    ve.wait_ge(up_done, 32 * it + (KT * gg + m + 1))
                    if not isinstance(it, int) or it > 0 or gg > 0:
                        ve.wait_ge(up_added, 32 * it + (KT * gg + m - 7))
                    tt(xT[:, m, :], bank[:, 2 + m % 4, :], xT[:, m, :], ALU.add).then_inc(up_added, 1)

            for e in range(2):
                weigh(0, e, 0, 1)
            for k in range(2):
                ve.wait_ge(p_hi_ready, k + 1)
                mark(tt(b_lo[:, 4 + k, :], pT[:, k, :], b_hi[:, 4 + k, :].bitcast(F32), ALU.subtract), p_split)

            def expert_step(it, last=False):
                for gg in range(4):
                    if not (last and gg == 3):
                        for c in range(2):
                            e8 = 2 * gg + 2 + c
                            weigh(it, e8, (e8 // 4) % 2, e8 // 8 + 1)
                    add_up(it, gg)

            expert_step(0)
            with ve.Fori(1, NKEY // 8 - 1) as it:
                expert_step(it)
            expert_step(NKEY // 8 - 1, last=True)
            ve.wait_ge(up_added, KT * NKEY // 2)

            norm(2)
            for m in range(KT):
                z = next_tile()
                ve.wait_ge(pproj_ready, m + 1)
                step(tt(prod, z, pproj[:, m, :], ALU.mult))
                ve.sem_inc(tile_free, 1)
                mark(tt(xT[:, m, :], xT[:, m, :], prod, ALU.add), x_ready)
            norm_scale(3)
            for k in range(KT):
                mark(stt(out=final[:, k, :], in0=xT[:, k, :], scalar=gains[:, 3, k:k + 1], in1=rrms,
                    op0=ALU.mult, op1=ALU.mult), final_ready)


def constants():
    f = np.float32

    def rope(dim):
        inv = (f(1.0) / np.power(f(10000.0), np.arange(0, dim, 2, dtype=f) / f(dim))).astype(f)
        ang = np.arange(S, dtype=f)[None, :] * inv[:, None]
        return np.cos(ang).astype(f), np.sin(ang).astype(f)

    c, s = rope(RDK)
    rope_r = np.stack([c, s], 1)
    c, s = rope(ADH)
    rope_a = np.stack([np.concatenate([c, c]), np.concatenate([-s, s])], 1)
    n = np.arange(S)[None, :] - np.arange(P)[:, None]
    decay = np.zeros((RH, P, S), f)
    for h in range(RH):
        gamma = np.log(1.0 - 2.0 ** (-5.0 - h))
        decay[h] = np.where(n >= 0, np.exp(gamma * np.maximum(n, 0)) * RDK ** -0.5, 0.0)
    q = np.arange(P)[:, None] // CHUNK
    k = np.arange(2 * P)[None, :] // CHUNK
    mask = np.zeros((P, TT, 2 * P), f)
    mask[:] = np.where((k == q + 1) | (k == q + 2), 0.0, NEG)[:, None, :]
    mask[:, 0, 0:P] = NEG
    eye = np.eye(P, dtype=f)
    fixed = np.concatenate([eye, np.roll(eye, P // 2, axis=1), np.ones((P, P), f),
                            np.broadcast_to(np.arange(P, dtype=f), (P, P))], 1)
    return rope_r, rope_a, decay, mask, fixed


def kernel(**inputs):
    import concourse.bacc as bacc
    from concourse.bass_utils import run_bass_kernel_spmd

    a = {k: np.asarray(v) for k, v in inputs.items()}
    rope_r, rope_a, decay, mask, fixed = constants()
    w_in = a["w_in"][0]

    def by_columns(w, first, n):
        return w[:, first:first + P * n].reshape(KT, P, n, P).transpose(2, 1, 0, 3).reshape(n, P, UW)

    wor = a["w_o_ret"][0].reshape(RH, 4, P, 4, 2 * P).transpose(0, 3, 2, 1, 4).reshape(4 * RH, P, UW)
    down = a["peer_down"][0].reshape(P, NKEY, KT, P).transpose(1, 3, 2, 0).reshape(NKEY, P, UW)
    up = a["peer_up"][0].reshape(P, NKEY, D).transpose(1, 0, 2)
    pp = a["w_ple_proj"][0].reshape(2, P, 2, 4 * P).transpose(2, 1, 0, 3).reshape(2, P, UW)
    kinds = {
        "aq": by_columns(w_in, AQ0, AH), "ak": by_columns(w_in, AK0, AKV), "av": by_columns(w_in, AV0, AKV),
        "rq": by_columns(w_in, RQ0, 2 * RH), "rk": by_columns(w_in, RK0, 2 * RH),
        "rv": by_columns(w_in, RV0, 4 * RH), "rg": by_columns(w_in, RG0, 4 * RH),
        "ga": by_columns(w_in, GA0, KT), "gr": by_columns(w_in, GR0, KT),
        "wor": wor, "woa": by_columns(a["w_o_att"][0], 0, KT), "out": by_columns(a["w_out"][0], 0, KT),
        "pq": by_columns(a["w_peer_query"][0], 0, 2 * PH), "dn": down, "up": up, "pp": pp,
        "pg": by_columns(a["w_ple_gate"][0], 0, KT),
    }
    weights = np.empty((NU, P, UW), np.float32)
    for n, (kind, i) in enumerate(UNITS):
        weights[n] = kinds[kind][i]

    def to_columns(x, tiles):
        return np.ascontiguousarray(x.reshape(S, tiles, P).transpose(2, 1, 0))

    gains = np.stack([a["mix_norm"][0], a["ffn_norm"][0], a["ple_norm"][0], a["final_norm"]])
    gains = gains.reshape(4, KT, P).transpose(2, 0, 1).reshape(P, 4 * KT)
    sinks = np.broadcast_to(a["attn_sinks"][0], (P, AH))
    sub_keys = a["peer_sub_keys"][0].transpose(2, 0, 1).reshape(P, 2 * NKEY)
    small = np.ascontiguousarray(np.concatenate([fixed, gains, sinks, sub_keys], 1))

    nc = bacc.Bacc("TRN2", target_bir_lowering=False, num_devices=1, dynamic_dma_scratch_size=1024)
    arrays = {
        "x_cols": to_columns(a["x"][0], KT), "weights": weights, "small_in": small, "rope_r": rope_r,
        "decay": decay, "rope_a": rope_a, "mask": mask, "p_cols": to_columns(a["p"][0, 0], 2),
    }
    args = [nc.dram_tensor(k, v.shape, F32, kind="ExternalInput").ap() for k, v in arrays.items()]
    args.append(nc.dram_tensor("outT", (P, KT, S), F32, kind="ExternalOutput").ap())
    block_program(nc, *args)
    r = run_bass_kernel_spmd(nc, [arrays], core_ids=[0])
    return r.results[0]["outT"].transpose(2, 1, 0).reshape(1, S, D)
```

```python
from contextlib import ExitStack

import numpy as np

import concourse.bass as bass
from concourse import mybir

F32 = mybir.dt.float32
F32R = mybir.dt.float32r
BF16 = mybir.dt.bfloat16
U32 = mybir.dt.uint32
ALU = mybir.AluOpType
ACT = mybir.ActivationFunctionType
AX_X = mybir.AxisListType.X

D, S, CHUNK, EPS = 1024, 512, 64, 1e-6
AH, AKV, ADH = 8, 2, 128
RH, RDK, RDV = 4, 256, 512
PH, NKEY, TOPK = 8, 128, 16
PLE = 256
NEG = -1e30
P = 128
KT = D // P
TT = S // P
SLOTS = PH * TOPK
LOWEST = -3.0e38

AQ0, AK0, AV0 = 0, AH * ADH, AH * ADH + AKV * ADH
RQ0 = AV0 + AKV * ADH
RK0, RV0 = RQ0 + RH * RDK, RQ0 + 2 * RH * RDK
RG0 = RV0 + RH * RDV
GA0 = RG0 + RH * RDV
GR0 = GA0 + D

UW = 1024
RAW = 4
RING = 8


def weight_units():
    u = []
    for i in range(RH + 1):
        if i < RH:
            u += [("rq", 2 * i), ("rq", 2 * i + 1), ("rk", 2 * i), ("rk", 2 * i + 1)]
        if i > 0:
            u += [("wor", 4 * (i - 1) + c) for c in range(4)]
        if i < RH:
            u += [("rv", 4 * i + c) for c in range(4)] + [("rg", 4 * i + c) for c in range(4)]
    u += [("gr", m) for m in range(KT)]
    u += [("ak", 0), ("ak", 1), ("av", 0), ("av", 1)]
    u += [("aq", h) for h in range(AH)]
    for m in range(KT):
        u += [("ga", m), ("woa", m)]
    u += [("out", m) for m in range(KT)]
    u += [("pq", m) for m in range(2 * PH)]
    u += [("dn", e) for e in range(NKEY)]
    u += [("up", e) for e in range(NKEY)]
    u += [("pp", 0), ("pp", 1)]
    u += [("pg", m) for m in range(KT)]
    return u


UNITS = weight_units()
NU = len(UNITS)
UNIT = {k: n for n, k in enumerate(UNITS)}
DN0, UP0 = UNIT[("dn", 0)], UNIT[("up", 0)]
LEAD = 5


def projection_outputs():
    o = []
    for i in range(RH + 1):
        if i < RH:
            o += [("rq", 2 * i), ("rq", 2 * i + 1), ("rk", 2 * i), ("rk", 2 * i + 1)]
        if i > 0:
            o += [("wor", i - 1, m) for m in range(KT)]
        if i < RH:
            o += [("rv", i, t) for t in range(TT)] + [("rg", i, t) for t in range(TT)]
    o += [("gr", m) for m in range(KT)]
    o += [("ak", 0), ("ak", 1)] + [("av", t) for t in range(TT)]
    o += [("aq", h) for h in range(AH)]
    for m in range(KT):
        o += [("ga", m), ("woa", m)]
    o += [("out", m) for m in range(KT)]
    o += [("pq", m) for m in range(2 * PH)]
    o += [("pp", m) for m in range(KT)]
    o += [("pg", m) for m in range(KT)]
    return o


OUT = {k: n for n, k in enumerate(projection_outputs())}
LAST_UNIT = {}
for _k in OUT:
    if _k[0] in ("rv", "rg"):
        LAST_UNIT[_k] = UNIT[(_k[0], 4 * _k[1] + 3)]
    elif _k[0] == "wor":
        LAST_UNIT[_k] = UNIT[("wor", 4 * _k[1] + _k[2] // 2)]
    elif _k[0] == "av":
        LAST_UNIT[_k] = UNIT[("av", 1)]
    elif _k[0] == "pp":
        LAST_UNIT[_k] = UNIT[("pp", _k[1] // 4)]
    else:
        LAST_UNIT[_k] = UNIT[_k]
USED_AT = {}
for _k, _n in OUT.items():
    if _k[0] in ("rv", "rg"):
        _units = range(LAST_UNIT[_k] - 3, LAST_UNIT[_k] + 1)
    elif _k[0] == "av":
        _units = range(LAST_UNIT[_k] - 1, LAST_UNIT[_k] + 1)
    else:
        _units = [LAST_UNIT[_k]]
    for _u in _units:
        USED_AT[_u] = _n

S_AT = [0, 512, 896, 1152]
SMALL = 808
SCRATCH = 15104

TG = 32
NTG = S // TG
JQ = 4
STEP = 8
FIRST_Z = 6



def block_program(nc, xT_d, w_d, small_d, rope_r_d, decay_d, rope_a_d, mask_d, pT_d, out_d):
    gate_d = nc.dram_tensor("gate_scratch", (NTG, P, NKEY * TG), F32, kind="Internal").ap()
    act_d = nc.dram_tensor("act_scratch", (NKEY // 2, P, 2 * S), F32, kind="Internal").ap()

    with ExitStack() as ctx:
        def sb(name, shape, dt=F32):
            return ctx.enter_context(nc.sbuf_tensor(name, shape, dt))

        def sem(name):
            return ctx.enter_context(nc.semaphore(name))

        xT = sb("xT", [P, KT, S])
        raw = sb("raw", [P, RAW, UW])
        w_hi = sb("w_hi", [P, RING, UW], F32R)
        w_lo = sb("w_lo", [P, RING, UW], F32R)
        h_hi = sb("h_hi", [P, KT, S], F32R)
        h_lo = sb("h_lo", [P, KT, S], F32R)
        b_hi = sb("b_hi", [P, KT, S], F32R)
        b_lo = sb("b_lo", [P, KT, S], F32R)
        small = sb("small", [P, SMALL])
        ident, swap, ones = small[:, 0:128], small[:, 128:256], small[:, 256:384]
        iota = small[:, 384:512]
        gains = small[:, 512:544].rearrange("p (n k) -> p n k", n=4)
        sinks = small[:, 544:552]
        sub_keys = small[:, 552:808].rearrange("p (a k) -> p a k", a=2)
        misc = sb("misc", [P, 128])
        scr = sb("scr", [P, SCRATCH])

        def cut(at, n):
            assert at + n <= SCRATCH, (at, n)
            return scr[:, at:at + n]

        def cut3(at, a, b):
            return cut(at, a * b).rearrange("p (a b) -> p a b", a=a)

        yacc = cut3(0, KT, S)
        tile2 = cut3(4096, 2, S)
        prod = cut(5120, S)
        sq = cut3(8704, 2, S)
        normed = cut3(9728, 2, S)
        rrms = cut(10752, S)
        rope_r = cut3(5632, 2, S)
        decay = cut3(6656, 2, S)
        r_q = cut3(7680, 2, S)
        r_k = cut3(8704, 2, S)
        r_v = cut3(9728, TT, RDV)
        r_g = cut3(11776, TT, RDV)
        r_s = cut(13824, 1280)
        stats = misc[:, 0:24].rearrange("p (t n) -> p t n", t=TT)
        mean_var = misc[:, 24:32].rearrange("p (t n) -> p t n", t=TT)
        var_eps, std4, rstd4 = misc[:, 32:36], misc[:, 36:40], misc[:, 40:44]
        a_k = cut3(5632, AKV, S)
        a_v = cut3(6656, TT, AKV * ADH)
        a_q = cut3(7680, 2, S)
        a_s = cut(8704, 2048).rearrange("p (b t k) -> p b t k", b=2, t=TT)
        a_pT = cut(10752, 1024).rearrange("p (t b q) -> p t b q", t=TT, b=2)
        rope_a = cut3(11776, 2, S)
        mask = cut(12800, 1024).rearrange("p (t k) -> p t k", t=TT)
        smax, negmax, psum4, esink, rden = (misc[:, 48 + 4 * n:52 + 4 * n] for n in range(5))
        s12 = cut(5632, 2048).rearrange("p (m t k) -> p m t k", m=4, t=TT)
        taken = cut(7680, 256)
        cand = cut(7936, 256)
        val = cut(9216, 1024).rearrange("p (t m k) -> p t m k", t=TT, m=2 * PH)
        idx = cut(10240, 1024).bitcast(U32).rearrange("p (t m k) -> p t m k", t=TT, m=2 * PH)
        idxf = cut(11264, 1024).rearrange("p (t m k) -> p t m k", t=TT, m=2 * PH)
        top = cut(2048, 512).rearrange("p (t h k) -> p t h k", t=TT, h=PH)
        pos = cut(2560, 512).bitcast(U32).rearrange("p (t h k) -> p t h k", t=TT, h=PH)
        posu = cut(3072, 512).bitcast(U32).rearrange("p (t h k) -> p t h k", t=TT, h=PH)
        posf = cut(3584, 512).rearrange("p (t h k) -> p t h k", t=TT, h=PH)
        pick = cut(0, 2048).rearrange("p (h k j) -> p h k j", h=PH, k=TOPK)
        row_s = cut(6144, 512).rearrange("p (t n) -> p t n", t=TT)
        col_s = cut(6656, 512).rearrange("p (t n) -> p t n", t=TT)
        gate_s = cut(7168, 512).rearrange("p (t n) -> p t n", t=TT)
        gsum = misc[:, 72:104]
        stage = cut(0, 8192).rearrange("p (b j t) -> p b j t", b=2, t=TG)
        rowT, colT, gateT = (cut(8192 + 512 * n, S).rearrange("p (g c) -> p g c", g=NTG) for n in range(3))
        onehot = cut(9728, 2048).rearrange("p (b q n k) -> p b q n k", b=2, q=4, n=2)
        act = cut3(13056, 4, S)
        gates = cut(0, 4096).rearrange("p (b g j t) -> p b g j t", b=2, g=NTG, j=JQ)
        acts = cut(4096, 4096).rearrange("p (b j t) -> p b j t", b=2, j=JQ)
        wgt = cut3(8192, 2, S)
        pT = cut3(11776, 2, S)
        pproj = cut3(0, KT, S)
        final = cut3(0, KT, S)

        bank = ctx.enter_context(nc.psum_tensor("bank", [P, 8, 512], F32))

        landed = [sem(f"landed{i}") for i in range(RAW)]
        hi_done = sem("hi_done")
        lo_done = sem("lo_done")
        z_done = sem("z_done")
        proj_done = sem("proj_done")
        proj_free = [sem("proj_free0"), sem("proj_free1")]
        x_landed, small_landed = sem("x_landed"), sem("small_landed")
        rope_r_landed, rope_a_landed, p_landed = sem("rope_r_landed"), sem("rope_a_landed"), sem("p_landed")
        decay_landed = [sem("decay_landed0"), sem("decay_landed1")]
        sq_ready, sq_used, ss_done = sem("sq_ready"), sem("sq_used"), sem("ss_done")
        ms_ready, rms_ready = sem("ms_ready"), sem("rms_ready")
        normed_ready, h_hi_ready, h_ready = sem("normed_ready"), sem("h_hi_ready"), sem("h_ready")
        x_ready = sem("x_ready")
        tile_ready, tile_free = sem("tile_ready"), sem("tile_free")
        rot_ready = sem("rot_ready")
        rs_done, rs_ready = sem("rs_done"), sem("rs_ready")
        rv_ready, rg_ready = sem("rv_ready"), sem("rg_ready")
        y_done, var_ready, std_ready, gn_done = sem("y_done"), sem("var_ready"), sem("std_ready"), sem("gn_done")
        tr_done, b_hi_ready, b_ready = sem("tr_done"), sem("b_hi_ready"), sem("b_ready")
        yacc_ready = sem("yacc_ready")
        swap_done, arot_done = sem("swap_done"), sem("arot_done")
        av_ready, sc_done, sc_read = sem("av_ready"), sem("sc_done"), sem("sc_read")
        max_ready, exp_ready, p_ready = sem("max_ready"), sem("exp_ready"), sem("p_ready")
        pt_done, pT_ready, pv_done = sem("pt_done"), sem("pT_ready"), sem("pv_done")
        ks_done, s12_ready, s12_free = sem("ks_done"), sem("s12_ready"), sem("s12_free")
        qp_ready = sem("qp_ready")
        top_ready, gexp_ready, sel_ready, selT_done = sem("top_ready"), sem("gexp_ready"), sem("sel_ready"), sem("selT_done")
        oh_ready, oh_used, stage_ready = sem("oh_ready"), sem("oh_used"), sem("stage_ready")
        gate_written = [sem("gate_written0"), sem("gate_written1")]
        gate_landed = [sem("gate_landed0"), sem("gate_landed1")]
        act_ready, wgt_ready, wgt_hi_ready, wgt_split = sem("act_ready"), sem("wgt_ready"), sem("wgt_hi_ready"), sem("wgt_split")
        up_done, up_added = sem("up_done"), sem("up_added")
        act_written = [sem("act_written0"), sem("act_written1")]
        acts_landed = [sem("acts_landed0"), sem("acts_landed1")]
        p_hi_ready, p_split, pproj_ready = sem("p_hi_ready"), sem("p_split"), sem("pproj_ready")
        final_ready, stored = sem("final_ready"), sem("stored")
        dve_step = sem("dve_step")

        block = ctx.enter_context(nc.Block())
        w_rounds = w_d[0:NU // RAW * RAW].rearrange("(r s) p n -> s r p n", s=RAW)
        gate_quads = gate_d.rearrange("g p (i b n) -> b i p g n", b=2, n=JQ * TG)
        act_quads = act_d.rearrange("(i b a) p n -> b i p a n", b=2, a=2)
        gate_pairs = gate_d.rearrange("(i b) p n -> b i p n", b=2)
        act_pairs = act_d.rearrange("(i a) p n -> a i p n", a=STEP // 2)

        def proj_bank(key):
            return bank[:, OUT[key] % 2, :]

        def wait_output(eng, key):
            eng.wait_ge(proj_done, OUT[key] + 1)

        def wait_used(eng, u):
            kind, e = UNITS[u]
            if kind == "dn":
                eng.wait_ge(z_done, e + 1)
            elif kind == "up":
                eng.wait_ge(up_done, e + 1)
            else:
                eng.wait_ge(proj_done, USED_AT[u] + 1)

        def free_of(key):
            return proj_free[OUT[key] % 2]

        @block.sync
        def _(sp):
            sp.dma_start(xT[:, :, :], xT_d).then_inc(x_landed, 16)
            sp.dma_start(small[:, :], small_d).then_inc(small_landed, 16)
            for s in range(RAW):
                sp.dma_start(raw[:, s, :], w_d[s]).then_inc(landed[s], 16)
            with sp.Fori(1, NU // RAW) as r:
                for s in range(RAW):
                    sp.wait_ge(lo_done, RAW * r + (s - RAW + 1))
                    sp.dma_start(raw[:, s, :], w_rounds[s][r]).then_inc(landed[s], 16)
            for u in range(NU // RAW * RAW, NU):
                sp.wait_ge(lo_done, u - RAW + 1)
                sp.dma_start(raw[:, u % RAW, :], w_d[u]).then_inc(landed[u % RAW], 16)
            for k in range(KT):
                sp.wait_ge(final_ready, k + 1)
                sp.dma_start(out_d[:, k, :], final[:, k, :]).then_inc(stored, 16)
            sp.wait_ge(stored, 16 * KT)

        @block.gpsimd
        def _(pool):
            def lower(s):
                return nc.gpsimd.tensor_tensor(w_lo[:, s, :], raw[:, s % RAW, :], w_hi[:, s, :].bitcast(F32),
                                               ALU.subtract)

            with pool.Fori(0, NU // RING) as r:
                for s in range(RING):
                    pool.wait_ge(hi_done, RING * r + (s + 1))
                    lower(s).then_inc(lo_done, 1)
            for u in range(NU // RING * RING, NU):
                pool.wait_ge(hi_done, u + 1)
                lower(u % RING).then_inc(lo_done, 1)

        @block.scalar
        def _(sc):
            ahead = [0]
            tiles = [0]

            def upper(u, u_mod):
                s = u_mod % RAW
                sc.wait_ge(landed[s], 4 * (u - s) + 16)
                if isinstance(u, int) and u >= RING:
                    wait_used(sc, u - RING)
                nc.scalar.activation(w_hi[:, u_mod, :], raw[:, s, :], ACT.Copy).then_inc(hi_done, 1)

            def run_ahead(u):
                while ahead[0] <= min(u, NU - 1):
                    upper(ahead[0], ahead[0] % RING)
                    ahead[0] += 1

            def output(key):
                whole = key[0] in ("rv", "rg", "av")
                run_ahead(LAST_UNIT[key] + (0 if whole else 4))
                wait_output(sc, key)
                return proj_bank(key)

            def to_tile(key, func):
                src = output(key)
                z = tiles[0]
                tiles[0] += 1
                if z >= 2:
                    sc.wait_ge(tile_free, z - 1)
                ins = nc.scalar.activation(tile2[:, z % 2, :], src, func)
                ins.then_inc(tile_ready, 1)
                sc.wait_ge(tile_ready, z + 1)
                sc.sem_inc(free_of(key), 1)

            def norm(r, ready):
                for k in range(KT):
                    ready(k)
                    n = KT * r + k
                    if n >= 2:
                        sc.wait_ge(sq_used, n - 1)
                    nc.scalar.activation(sq[:, k % 2, :], xT[:, k, :], ACT.Square).then_inc(sq_ready, 1)
                sc.wait_ge(ms_ready, r + 1)
                nc.scalar.activation(rrms, rrms, ACT.Sqrt).then_inc(rms_ready, 1)

            def norm_upper(r):
                for k in range(KT):
                    sc.wait_ge(normed_ready, KT * r + k + 1)
                    nc.scalar.activation(h_hi[:, k, :], normed[:, k % 2, :], ACT.Copy).then_inc(h_hi_ready, 1)

            sc.dma_start(rope_r[:, :, :], rope_r_d).then_inc(rope_r_landed, 16)
            for i in range(2):
                sc.dma_start(decay[:, i, :], decay_d[i]).then_inc(decay_landed[i], 16)
            run_ahead(3)
            sc.wait_ge(x_landed, 16)
            sc.wait_ge(small_landed, 16)
            norm(0, lambda k: None)
            norm_upper(0)

            for i in range(RH + 1):
                if i < RH:
                    for key in (("rq", 2 * i), ("rq", 2 * i + 1), ("rk", 2 * i), ("rk", 2 * i + 1)):
                        to_tile(key, ACT.Copy)
                if i > 0:
                    for c in range(4):
                        sc.wait_ge(tr_done, 4 * (i - 1) + c + 1)
                        nc.scalar.activation(b_hi[:, c, :], bank[:, 6 + c % 2, :], ACT.Copy).then_inc(b_hi_ready, 1)
                    if 1 < i + 1 < RH:
                        sc.wait_ge(rs_ready, 4 * i)
                        sc.dma_start(decay[:, (i + 1) % 2, :], decay_d[i + 1]).then_inc(decay_landed[(i + 1) % 2], 16)
                if i < RH:
                    for t in range(TT):
                        src = output(("rv", i, t))
                        if i > 0 and t == 0:
                            sc.wait_ge(y_done, TT * i)
                        nc.scalar.activation(r_v[:, t, :], src, ACT.Copy).then_inc(rv_ready, 1)
                        sc.wait_ge(rv_ready, TT * i + t + 1)
                        sc.sem_inc(free_of(("rv", i, t)), 1)
                    for t in range(TT):
                        src = output(("rg", i, t))
                        nc.scalar.activation(r_g[:, t, :], src, ACT.Silu).then_inc(rg_ready, 1)
                        sc.wait_ge(rg_ready, TT * i + t + 1)
                        sc.sem_inc(free_of(("rg", i, t)), 1)
                    sc.wait_ge(var_ready, i + 1)
                    nc.scalar.activation(std4, var_eps, ACT.Sqrt).then_inc(std_ready, 1)
            sc.wait_ge(tr_done, 4 * RH)
            sc.dma_start(rope_a[:, :, :], rope_a_d).then_inc(rope_a_landed, 16)
            sc.dma_start(mask, mask_d).then_inc(rope_a_landed, 16)
            for m in range(KT):
                to_tile(("gr", m), ACT.Sigmoid)

            to_tile(("ak", 0), ACT.Copy)
            to_tile(("ak", 1), ACT.Copy)
            for t in range(TT):
                src = output(("av", t))
                nc.scalar.activation(a_v[:, t, :], src[:, 0:AKV * ADH], ACT.Copy).then_inc(av_ready, 1)
                sc.wait_ge(av_ready, t + 1)
                sc.sem_inc(free_of(("av", t)), 1)
            for i in range(AH + 4):
                if i < AH:
                    to_tile(("aq", i), ACT.Copy)
                if 0 <= i - 2 < AH:
                    h = i - 2
                    sc.wait_ge(max_ready, h + 1)
                    for t in range(TT):
                        nc.scalar.activation(a_s[:, h % 2, t, :], a_s[:, h % 2, t, :], ACT.Exp,
                                             bias=negmax[:, t:t + 1], accum_out=psum4[:, t:t + 1])
                    nc.scalar.activation(esink, negmax, ACT.Exp, bias=sinks[:, h:h + 1]).then_inc(exp_ready, 1)
                if 0 <= i - 3 < AH:
                    h = i - 3
                    sc.wait_ge(pt_done, h + 1)
                    if h > 0:
                        sc.wait_ge(pv_done, h)
                    nc.scalar.activation(a_pT.rearrange("p t b q -> p (t b q)"),
                                         bank[:, 5:7, :].rearrange("p a b -> p (a b)"), ACT.Copy).then_inc(pT_ready, 1)
                if 0 <= i - 4 < AH:
                    h = i - 4
                    sc.wait_ge(pv_done, h + 1)
                    nc.scalar.activation(b_hi[:, h, :], bank[:, 7, :], ACT.Copy).then_inc(b_hi_ready, 1)
            for m in range(KT):
                to_tile(("ga", m), ACT.Sigmoid)
            run_ahead(UNIT[("woa", KT - 1)] + 4)
            wait_output(sc, ("woa", KT - 1))
            for m in range(KT):
                sc.wait_ge(yacc_ready, RH * KT + m + 1)
                nc.scalar.activation(h_hi[:, m, :], yacc[:, m, :], ACT.Copy).then_inc(h_hi_ready, 1)
            run_ahead(UNIT[("out", KT - 1)])
            norm(1, lambda k: sc.wait_ge(x_ready, k + 1))
            for k in range(KT):
                sc.wait_ge(normed_ready, KT + k + 1)
                nc.scalar.activation(h_hi[:, k, :], normed[:, k % 2, :], ACT.Copy).then_inc(h_hi_ready, 1)

            def key_scores(m):
                sc.wait_ge(ks_done, m + 1)
                if m >= 4:
                    sc.wait_ge(s12_free, m - 3)
                nc.scalar.activation(s12[:, m % 4].rearrange("p t k -> p (t k)"), bank[:, 2 + m % 2, :],
                                     ACT.Copy).then_inc(s12_ready, 1)

            for m in range(2 * PH):
                src = output(("pq", m))
                if m >= 2:
                    sc.wait_ge(ks_done, m - 1)
                nc.scalar.activation(tile2[:, m % 2, :], src, ACT.Copy).then_inc(qp_ready, 1)
                sc.wait_ge(qp_ready, m + 1)
                sc.sem_inc(free_of(("pq", m)), 1)
                if m > 0:
                    key_scores(m - 1)
            key_scores(2 * PH - 1)

            run_ahead(DN0 + LEAD - 1)

            def gelu(i, c):
                e = STEP * i + c
                u = DN0 + LEAD + e
                if isinstance(i, int) and i == 0:
                    upper(u, u % RING)
                else:
                    sc.wait_ge(z_done, e - (RING - LEAD - 1))
                    upper(u, (DN0 + LEAD + c) % RING)
                sc.wait_ge(z_done, e + 1)
                if c % 2 == 0 and not (isinstance(i, int) and STEP * i + c < 4):
                    sc.wait_ge(act_written[c // 2 % 2], 32 * i + 16 * (c // 4))
                nc.scalar.activation(act[:, c % 4, :], bank[:, c % 2, :], ACT.Gelu_apprx_tanh).then_inc(act_ready, 1)
                if c % 2 == 1:
                    sc.wait_ge(act_ready, e + 1)
                    sc.dma_start(act_pairs[c // 2][i], act[:, c % 4 - 1:c % 4 + 1, :].rearrange("p a t -> p (a t)")).then_inc(
                        act_written[c // 2 % 2], 16)

            def move_gates(j, q):
                b = q // (TG // 4)
                if q % (TG // 4) == 0 and not isinstance(j, int):
                    sc.wait_ge(gate_written[b], 16 * j)
                sc.wait_ge(oh_used, 16 * j + (q + 1))
                t = 4 * (q % (TG // 4))
                nc.scalar.activation(stage[:, b, :, t:t + 4].rearrange("p j t -> p t j"),
                                     bank[:, 2 + q % 4, :].rearrange("p (t j) -> p t j", t=4),
                                     ACT.Copy).then_inc(stage_ready, 1)
                if q % (TG // 4) == TG // 4 - 1:
                    sc.wait_ge(stage_ready, 16 * j + (q + 1))
                    sc.dma_start(gate_pairs[b][j], stage[:, b].rearrange("p j t -> p (j t)")).then_inc(gate_written[b], 16)

            def gelu_turn(i):
                for c in range(STEP):
                    gelu(i, c)

            def read_back(i, b):
                sc.dma_start(gates[:, b].rearrange("p g j t -> p g (j t)"), gate_quads[b][i]).then_inc(gate_landed[b], 16)
                for par in range(2):
                    sc.wait_ge(act_written[par], 32 * i + 16 * (b + 1))
                sc.dma_start(acts[:, b].rearrange("p (a j) t -> p a (j t)", a=2), act_quads[b][i]).then_inc(acts_landed[b], 16)

            def gate_turn(j):
                for c in range(STEP):
                    gelu(j + (FIRST_Z + 1), c)
                    move_gates(j, 2 * c)
                    move_gates(j, 2 * c + 1)

            gelu_turn(0)
            gelu_turn(1)
            sc.wait_ge(top_ready, 1)
            nc.scalar.activation(gate_s.rearrange("p t n -> p (t n)"), gate_s.rearrange("p t n -> p (t n)"),
                                 ACT.Exp).then_inc(gexp_ready, 1)
            with sc.Fori(2, FIRST_Z + 1) as i:
                gelu_turn(i)
            gate_turn(0)
            sc.dma_start(pT[:, :, :], pT_d).then_inc(p_landed, 16)
            with sc.Fori(1, NTG // 2) as j:
                gate_turn(j)
            sc.wait_ge(p_landed, 16)
            for k in range(2):
                nc.scalar.activation(b_hi[:, 4 + k, :], pT[:, k, :], ACT.Copy).then_inc(p_hi_ready, 1)
            for c in range(STEP):
                gelu(NKEY // STEP - 1, c)
                if c == 2:
                    for b in range(2):
                        sc.wait_ge(gate_written[b], 16 * (NTG // 2))
                    read_back(0, 0)
                    read_back(0, 1)

            AHEAD = 2

            def weight_upper(e, c):
                sc.wait_ge(wgt_ready, e + 1)
                if not isinstance(e, int) or e >= 4:
                    sc.wait_ge(up_done, e - 3)
                nc.scalar.activation(b_hi[:, c % 4, :], wgt[:, c % 2, :], ACT.Copy).then_inc(wgt_hi_ready, 1)

            def up_turn(i):
                last = isinstance(i, int) and i > 0
                for c in range(STEP):
                    e = STEP * i + c
                    if isinstance(i, int):
                        upper(UP0 + LEAD + e, (UP0 + LEAD + e) % RING)
                    else:
                        sc.wait_ge(up_done, e - (RING - LEAD - 1))
                        upper(UP0 + LEAD + e, (UP0 + LEAD + c) % RING)
                    if not last or c + AHEAD < STEP:
                        weight_upper(e + AHEAD, (c + AHEAD) % STEP)
                    if not last and c % JQ == JQ - 1:
                        sc.wait_ge(wgt_ready, e + 1)
                        read_back(i + 1, c // JQ)

            for e in range(AHEAD):
                weight_upper(e, e)
            up_turn(0)
            with sc.Fori(1, NKEY // STEP - 1) as i:
                up_turn(i)
            up_turn(NKEY // STEP - 1)
            ahead[0] = UP0 + NKEY + LEAD

            for m in range(KT):
                src = output(("pp", m))
                if m == 0:
                    sc.wait_ge(wgt_ready, NKEY)
                nc.scalar.activation(pproj[:, m, :], src, ACT.Copy).then_inc(pproj_ready, 1)
                sc.wait_ge(pproj_ready, m + 1)
                sc.sem_inc(free_of(("pp", m)), 1)
            norm(2, lambda k: sc.wait_ge(up_added, k + 1))
            for k in range(KT):
                sc.wait_ge(normed_ready, 2 * KT + k + 1)
                nc.scalar.activation(h_hi[:, k, :], normed[:, k % 2, :], ACT.Copy).then_inc(h_hi_ready, 1)
            for m in range(KT):
                to_tile(("pg", m), ACT.Sigmoid)
            norm(3, lambda k: sc.wait_ge(x_ready, KT + k + 1))

        @block.tensor
        def _(pe):
            def mm3(out, a_hi, a_lo, c_hi, c_lo, first, last):
                nc.tensor.matmul(out, a_hi, c_hi, start=first, stop=False)
                nc.tensor.matmul(out, a_hi, c_lo, start=False, stop=False)
                return nc.tensor.matmul(out, a_lo, c_hi, start=False, stop=last)

            def bank_free(key):
                n = OUT[key]
                if n >= 2:
                    pe.wait_ge(proj_free[n % 2], n // 2)

            def columns(key, r_hi, r_lo, kt=KT, u=None, at=0, width=P):
                u = UNIT[key] if u is None else u
                pe.wait_ge(lo_done, u + 1)
                bank_free(key)
                s = u % RING
                for k in range(kt):
                    o = k * width + at
                    ins = mm3(proj_bank(key), w_hi[:, s, o:o + P], w_lo[:, s, o:o + P],
                              r_hi[:, k, :], r_lo[:, k, :], k == 0, k == kt - 1)
                ins.then_inc(proj_done, 1)

            def tokens(keys, kind, u0, nu):
                pe.wait_ge(lo_done, u0 + nu)
                s = u0 % RING
                assert s + nu <= RING
                for t, key in enumerate(keys):
                    bank_free(key)
                    o = proj_bank(key)[:, 0:nu * P]
                    for k in range(KT):
                        ins = mm3(o, h_hi[:, k, P * t:P * t + P], h_lo[:, k, P * t:P * t + P],
                                  w_hi[:, s:s + nu, k * P:k * P + P], w_lo[:, s:s + nu, k * P:k * P + P],
                                  k == 0, k == KT - 1)
                    ins.then_inc(proj_done, 1)

            def norm(r):
                for k in range(KT):
                    pe.wait_ge(sq_ready, KT * r + k + 1)
                    ins = nc.tensor.matmul(bank[:, 7, :], ones, sq[:, k % 2, :], start=k == 0, stop=k == KT - 1)
                    ins.then_inc(sq_used, 1)

            pe.wait_ge(small_landed, 16)
            norm(0)
            pe.wait_ge(h_ready, KT)
            for i in range(RH + 1):
                if i < RH:
                    for key in (("rq", 2 * i), ("rq", 2 * i + 1), ("rk", 2 * i), ("rk", 2 * i + 1)):
                        columns(key, h_hi, h_lo)
                if i > 0:
                    pe.wait_ge(gn_done, TT * i)
                    for c in range(4):
                        n = 4 * (i - 1) + c
                        if n >= 2:
                            pe.wait_ge(b_ready, n - 1)
                        for t in range(TT):
                            ins = nc.tensor.transpose(bank[:, 6 + c % 2, P * t:P * t + P],
                                                      r_g[:, t, P * c:P * c + P], ident)
                        ins.then_inc(tr_done, 1)
                    pe.wait_ge(b_ready, 4 * i)
                    for m in range(KT):
                        columns(("wor", i - 1, m), b_hi, b_lo, kt=4, u=UNIT[("wor", 4 * (i - 1) + m // 2)],
                                at=P * (m % 2), width=2 * P)
                if i < RH:
                    tokens([("rv", i, t) for t in range(TT)], "rv", UNIT[("rv", 4 * i)], 4)
                    pe.wait_ge(rot_ready, 2 * i + 2)
                    if i > 0:
                        pe.wait_ge(gn_done, TT * i)
                    for j in range(TT):
                        for c in range(2):
                            ins = nc.tensor.matmul(bank[:, 2 + j, 0:S - P * j], r_k[:, c, P * j:P * j + P],
                                                   r_q[:, c, P * j:S], start=c == 0, stop=c == 1)
                        ins.then_inc(rs_done, 1)
                    tokens([("rg", i, t) for t in range(TT)], "rg", UNIT[("rg", 4 * i)], 4)
                    pe.wait_ge(rs_ready, TT * (i + 1))
                    pe.wait_ge(rv_ready, TT * (i + 1))
                    for t in range(TT):
                        for j in range(t + 1):
                            o = S_AT[j] + P * (t - j)
                            ins = nc.tensor.matmul(bank[:, 2 + t, :], r_s[:, o:o + P], r_v[:, j, :],
                                                   start=j == 0, stop=j == t)
                        ins.then_inc(y_done, 1)
            for m in range(KT):
                columns(("gr", m), h_hi, h_lo)

            def swap_halves(r, z):
                pe.wait_ge(tile_ready, z + 1)
                if r > 0:
                    pe.wait_ge(arot_done, r)
                nc.tensor.matmul(bank[:, 2, :], swap, tile2[:, z % 2, :], start=True, stop=True).then_inc(swap_done, 1)

            z0 = 4 * RH + KT
            columns(("ak", 0), h_hi, h_lo)
            columns(("ak", 1), h_hi, h_lo)
            swap_halves(0, z0)
            tokens([("av", t) for t in range(TT)], "av", UNIT[("av", 0)], 2)
            swap_halves(1, z0 + 1)
            for i in range(AH + 4):
                if i < AH:
                    columns(("aq", i), h_hi, h_lo)
                if 1 <= i <= AH:
                    swap_halves(i + 1, z0 + i + 1)
                if 0 <= i - 2 < AH:
                    h = i - 2
                    kv = h // (AH // AKV)
                    pe.wait_ge(arot_done, h + 3)
                    if h > 0:
                        pe.wait_ge(sc_read, h)
                    for t in range(TT):
                        o = bank[:, 3 + t // 2, 256 * (t % 2):256 * (t % 2) + 256]
                        q = a_q[:, h % 2, P * t:P * t + P]
                        if t == 0:
                            nc.tensor.matmul(o[:, 0:P], q, a_k[:, kv, 0:P], start=True, stop=True)
                            nc.tensor.matmul(o[:, P:2 * P], q, a_k[:, kv, 0:P], start=True, stop=True)
                        else:
                            ins = nc.tensor.matmul(o, q, a_k[:, kv, P * (t - 1):P * (t + 1)], start=True, stop=True)
                    ins.then_inc(sc_done, 1)
                if 0 <= i - 3 < AH:
                    h = i - 3
                    pe.wait_ge(p_ready, h + 1)
                    if h > 0:
                        pe.wait_ge(pT_ready, h)
                    for t in range(TT):
                        for b in range(2):
                            o = ((t % 2) * 2 + b) * P
                            ins = nc.tensor.transpose(bank[:, 5 + t // 2, o:o + P],
                                                      a_s[:, h % 2, t, P * b:P * b + P], ident)
                    ins.then_inc(pt_done, 1)
                if 0 <= i - 4 < AH:
                    h = i - 4
                    kv = h // (AH // AKV)
                    pe.wait_ge(pT_ready, h + 1)
                    pe.wait_ge(av_ready, TT)
                    if h > 0:
                        pe.wait_ge(b_ready, 4 * RH + h)
                    for t in range(TT):
                        for b in range(2):
                            if t == 0 and b == 0:
                                continue
                            ins = nc.tensor.matmul(bank[:, 7, P * t:P * t + P], a_v[:, t - 1 + b, P * kv:P * kv + P],
                                                   a_pT[:, t, b, :], start=b == 0 or t == 0, stop=b == 1)
                    ins.then_inc(pv_done, 1)
            for m in range(KT):
                columns(("ga", m), h_hi, h_lo)
                if m == 0:
                    pe.wait_ge(b_ready, 4 * RH + AH)
                columns(("woa", m), b_hi, b_lo)
            pe.wait_ge(h_ready, 2 * KT)
            for m in range(KT):
                columns(("out", m), h_hi, h_lo)
            norm(1)
            pe.wait_ge(h_ready, 3 * KT)

            def key_scores(m):
                pe.wait_ge(qp_ready, m + 1)
                if m >= 2:
                    pe.wait_ge(s12_ready, m - 1)
                for t in range(TT):
                    ins = nc.tensor.matmul(bank[:, 2 + m % 2, P * t:P * t + P], tile2[:, m % 2, P * t:P * t + P],
                                           sub_keys[:, m % 2, :], start=True, stop=True)
                ins.then_inc(ks_done, 1)

            for m in range(2 * PH):
                columns(("pq", m), h_hi, h_lo)
                if m > 0:
                    key_scores(m - 1)
            key_scores(2 * PH - 1)

            def down(i, c):
                e = STEP * i + c
                pe.wait_ge(lo_done, e + (DN0 + 1))
                if isinstance(i, int) and i == 0 and c < 2:
                    pe.wait_ge(proj_free[c], (OUT[("pp", 0)] + 1 - c) // 2)
                else:
                    pe.wait_ge(act_ready, e - 1)
                s = (DN0 + c) % RING
                for k in range(KT):
                    ins = mm3(bank[:, c % 2, :], w_hi[:, s, P * k:P * k + P], w_lo[:, s, P * k:P * k + P],
                              h_hi[:, k, :], h_lo[:, k, :], k == 0, k == KT - 1)
                ins.then_inc(z_done, 1)

            def down_turn(i):
                for c in range(STEP):
                    down(i, c)

            def scatter(j, q):
                pe.wait_ge(oh_ready, 16 * j + (q + 1))
                if not (isinstance(j, int) and q < 4):
                    pe.wait_ge(stage_ready, 16 * j + (q - 3))
                for x in range(4):
                    ins = nc.tensor.matmul(bank[:, 2 + q % 4, P * x:P * x + P], onehot[:, q % 2, x, 0, :],
                                           onehot[:, q % 2, x, 1, :], start=True, stop=True)
                ins.then_inc(oh_used, 1)

            def scatter_turn(j):
                for c in range(STEP):
                    down(j + (FIRST_Z + 1), c)
                    scatter(j, 2 * c)
                    scatter(j, 2 * c + 1)

            down_turn(0)
            with pe.Fori(1, FIRST_Z) as i:
                down_turn(i)
            pe.wait_ge(s12_ready, 2 * PH)
            pe.wait_ge(sel_ready, 1)
            for n, src in enumerate((row_s, col_s, gate_s)):
                for t in range(TT):
                    ins = nc.tensor.transpose(bank[:, 4 + n, P * t:P * t + P], src[:, t, :], ident)
            ins.then_inc(selT_done, 1)
            down_turn(FIRST_Z)
            scatter_turn(0)
            with pe.Fori(1, NTG // 2) as j:
                scatter_turn(j)
            down_turn(NKEY // STEP - 1)

            pe.wait_ge(act_ready, NKEY)
            pe.wait_ge(stage_ready, S // 4)

            def up(i, c):
                e = STEP * i + c
                pe.wait_ge(lo_done, e + (UP0 + 1))
                pe.wait_ge(wgt_split, e + 1)
                first = isinstance(i, int) and i == 0 and c == 0
                last = isinstance(i, int) and i > 0 and c == STEP - 1
                s = (UP0 + c) % RING
                for m in range(KT):
                    ins = mm3(bank[:, m, :], w_hi[:, s, P * m:P * m + P], w_lo[:, s, P * m:P * m + P],
                              b_hi[:, c % 4, :], b_lo[:, c % 4, :], first, last)
                ins.then_inc(up_done, 1)

            def up_turn(i):
                for c in range(STEP):
                    up(i, c)

            up_turn(0)
            with pe.Fori(1, NKEY // STEP - 1) as i:
                up_turn(i)
            up_turn(NKEY // STEP - 1)

            pe.wait_ge(up_added, 2)
            pe.wait_ge(p_split, 2)
            for m in range(KT):
                columns(("pp", m), b_hi[:, 4:6], b_lo[:, 4:6], kt=2, u=UNIT[("pp", m // 4)], at=P * (m % 4),
                        width=4 * P)
            pe.wait_ge(up_added, KT)
            norm(2)
            pe.wait_ge(h_ready, 4 * KT)
            for m in range(KT):
                columns(("pg", m), h_hi, h_lo)
            norm(3)

        @block.vector
        def _(ve):
            steps = [0]
            tiles = [0]

            def step(ins):
                steps[0] += 1
                ins.then_inc(dve_step, 1)
                ve.wait_ge(dve_step, steps[0])

            counts = {}

            def mark(ins, signal):
                counts[signal.name] = counts.get(signal.name, 0) + 1
                ins.then_inc(signal, 1)
                ve.wait_ge(signal, counts[signal.name])

            tt, ts, stt = nc.vector.tensor_tensor, nc.vector.tensor_scalar, nc.vector.scalar_tensor_tensor

            def norm_scale(r):
                ve.wait_ge(sq_used, KT * (r + 1))
                mark(ts(rrms, bank[:, 7, :], 1.0 / D, EPS, ALU.mult, ALU.add), ms_ready)
                ve.wait_ge(rms_ready, r + 1)
                step(nc.vector.reciprocal(rrms, rrms))

            def norm(r):
                norm_scale(r)
                hb = {0: 0, 1: 2 * KT, 2: 3 * KT}[r]
                for k in range(KT):
                    mark(stt(out=normed[:, k % 2, :], in0=xT[:, k, :], scalar=gains[:, r, k:k + 1], in1=rrms,
                        op0=ALU.mult, op1=ALU.mult), normed_ready)
                    ve.wait_ge(h_hi_ready, hb + k + 1)
                    mark(tt(h_lo[:, k, :], normed[:, k % 2, :], h_hi[:, k, :].bitcast(F32), ALU.subtract), h_ready)

            def next_tile():
                z = tiles[0]
                tiles[0] += 1
                ve.wait_ge(tile_ready, z + 1)
                return tile2[:, z % 2, :]

            ve.wait_ge(x_landed, 16)
            ve.wait_ge(small_landed, 16)
            norm(0)

            def rotate_pair(dst):
                z1, z2 = next_tile(), next_tile()
                c, s = rope_r[:, 0, :], rope_r[:, 1, :]
                step(tt(dst[:, 0, :], z1, c, ALU.mult))
                step(tt(prod, z2, s, ALU.mult))
                step(tt(dst[:, 0, :], dst[:, 0, :], prod, ALU.subtract))
                mark(tt(prod, z1, s, ALU.mult), tile_free)
                step(tt(dst[:, 1, :], z2, c, ALU.mult))
                ve.sem_inc(tile_free, 1)
                mark(tt(dst[:, 1, :], dst[:, 1, :], prod, ALU.add), rot_ready)

            ve.wait_ge(rope_r_landed, 16)
            for i in range(RH + 1):
                if i < RH:
                    if i > 0:
                        ve.wait_ge(rs_done, TT * i)
                    rotate_pair(r_q)
                    rotate_pair(r_k)
                if i > 0:
                    for c in range(4):
                        n = 4 * (i - 1) + c
                        ve.wait_ge(b_hi_ready, n + 1)
                        mark(tt(b_lo[:, c, :], bank[:, 6 + c % 2, :], b_hi[:, c, :].bitcast(F32),
                           ALU.subtract), b_ready)
                    for m in range(KT):
                        key = ("wor", i - 1, m)
                        wait_output(ve, key)
                        if i == 1:
                            ins = nc.vector.tensor_copy(yacc[:, m, :], proj_bank(key))
                        else:
                            ins = tt(yacc[:, m, :], proj_bank(key), yacc[:, m, :], ALU.add)
                        mark(ins, yacc_ready)
                        ve.sem_inc(free_of(key), 1)
                if i < RH:
                    ve.wait_ge(decay_landed[i % 2], 16 * (i // 2 + 1))
                    if i > 0:
                        ve.wait_ge(y_done, TT * i)
                    for j in range(TT):
                        ve.wait_ge(rs_done, TT * i + j + 1)
                        n = S - P * j
                        mark(tt(r_s[:, S_AT[j]:S_AT[j] + n], bank[:, 2 + j, 0:n], decay[:, i % 2, 0:n],
                           ALU.mult), rs_ready)
                    for t in range(TT):
                        ve.wait_ge(y_done, TT * i + t + 1)
                        step(nc.vector.bn_stats(stats[:, t, :], bank[:, 2 + t, :]))
                        step(nc.vector.bn_aggr(mean_var[:, t, :], stats[:, t, :]))
                    mark(ts(var_eps, mean_var[:, :, 1], EPS, None, ALU.add), var_ready)
                    ve.wait_ge(std_ready, i + 1)
                    step(nc.vector.reciprocal(rstd4, std4))
                    ve.wait_ge(rg_ready, TT * (i + 1))
                    for t in range(TT):
                        step(stt(out=r_g[:, t, :], in0=bank[:, 2 + t, :], scalar=mean_var[:, t, 0:1],
                                 in1=r_g[:, t, :], op0=ALU.subtract, op1=ALU.mult))
                        mark(ts(r_g[:, t, :], r_g[:, t, :], rstd4[:, t:t + 1], None, ALU.mult), gn_done)
            for m in range(KT):
                z = next_tile()
                mark(tt(yacc[:, m, :], yacc[:, m, :], z, ALU.mult), tile_free)

            ve.wait_ge(rope_a_landed, 32)

            def rotate(r, dst):
                z = next_tile()
                ve.wait_ge(swap_done, r + 1)
                step(tt(prod, bank[:, 2, :], rope_a[:, 1, :], ALU.mult))
                step(tt(dst, z, rope_a[:, 0, :], ALU.mult))
                step(tt(dst, dst, prod, ALU.add))
                ve.sem_inc(tile_free, 1)
                ve.sem_inc(arot_done, 1)

            rotate(0, a_k[:, 0, :])
            rotate(1, a_k[:, 1, :])
            for i in range(1, AH + 4):
                if i <= AH:
                    h = i - 1
                    if h >= 2:
                        ve.wait_ge(sc_done, h - 1)
                    rotate(h + 2, a_q[:, h % 2, :])
                if 0 <= i - 2 < AH:
                    h = i - 2
                    ve.wait_ge(sc_done, h + 1)
                    if h >= 2:
                        ve.wait_ge(pt_done, h - 1)
                    step(stt(out=a_s[:, h % 2].rearrange("p t k -> p (t k)"),
                             in0=bank[:, 3:5, :].rearrange("p a b -> p (a b)"), scalar=float(ADH) ** -0.5,
                             in1=mask.rearrange("p t k -> p (t k)"), op0=ALU.mult, op1=ALU.add))
                    ve.sem_inc(sc_read, 1)
                    step(nc.vector.tensor_reduce(smax, a_s[:, h % 2], AX_X, ALU.max))
                    step(ts(smax, smax, sinks[:, h:h + 1], None, ALU.max))
                    mark(ts(negmax, smax, -1.0, None, ALU.mult), max_ready)
                    ve.wait_ge(exp_ready, h + 1)
                    step(tt(rden, psum4, esink, ALU.add))
                    step(nc.vector.reciprocal(rden, rden))
                    for t in range(TT):
                        step(ts(a_s[:, h % 2, t, :], a_s[:, h % 2, t, :], rden[:, t:t + 1], None, ALU.mult))
                    ve.sem_inc(p_ready, 1)
                if 0 <= i - 4 < AH:
                    h = i - 4
                    ve.wait_ge(b_hi_ready, 4 * RH + h + 1)
                    mark(tt(b_lo[:, h, :], bank[:, 7, :], b_hi[:, h, :].bitcast(F32), ALU.subtract), b_ready)
            for m in range(KT):
                z = next_tile()
                key = ("woa", m)
                wait_output(ve, key)
                step(tt(prod, proj_bank(key), z, ALU.mult))
                ve.sem_inc(tile_free, 1)
                ve.sem_inc(free_of(key), 1)
                mark(tt(yacc[:, m, :], yacc[:, m, :], prod, ALU.add), yacc_ready)
            for m in range(KT):
                ve.wait_ge(h_hi_ready, KT + m + 1)
                mark(tt(h_lo[:, m, :], yacc[:, m, :], h_hi[:, m, :].bitcast(F32), ALU.subtract), h_ready)
            for m in range(KT):
                key = ("out", m)
                wait_output(ve, key)
                mark(tt(xT[:, m, :], proj_bank(key), xT[:, m, :], ALU.add), x_ready)
                ve.sem_inc(free_of(key), 1)
            norm(1)

            def best(src, values, places):
                step(nc.vector.max(values[:, 0:8], src))
                step(nc.vector.max_index(places[:, 0:8], values[:, 0:8], src))
                rest = taken[:, 0:src.shape[-1]]
                step(nc.vector.match_replace(rest, values[:, 0:8], src, LOWEST))
                step(nc.vector.max(values[:, 8:16], rest))
                return nc.vector.max_index(places[:, 8:16], values[:, 8:16], rest)

            for m in range(2 * PH):
                ve.wait_ge(s12_ready, m + 1)
                for t in range(TT):
                    step(best(s12[:, m % 4, t, :], val[:, t, m, :], idx[:, t, m, :]))
                ve.sem_inc(s12_free, 1)
                if m % 2 == 1:
                    h = m // 2
                    for t in range(TT):
                        step(tt(cand.rearrange("p (a b) -> p a b", a=TOPK),
                                val[:, t, m - 1, :].unsqueeze(2).to_broadcast([P, TOPK, TOPK]),
                                val[:, t, m, :].unsqueeze(1).to_broadcast([P, TOPK, TOPK]), ALU.add))
                        step(best(cand, top[:, t, h, :], pos[:, t, h, :]))
            g4 = gate_s.rearrange("p t (h k) -> p (t h) k", h=PH)
            top3 = top.rearrange("p t h k -> p (t h) k")
            ve.wait_ge(s12_ready, 2 * PH)
            mark(tt(g4, top3, top3[:, :, 0:1].to_broadcast([P, TT * PH, TOPK]), ALU.subtract), top_ready)
            step(nc.vector.tensor_copy(idxf, idx))
            ve.wait_ge(gexp_ready, 1)
            step(nc.vector.tensor_reduce(gsum, g4, AX_X, ALU.add))
            step(nc.vector.reciprocal(gsum, gsum))
            step(tt(g4, g4, gsum.unsqueeze(2).to_broadcast([P, TT * PH, TOPK]), ALU.mult))
            for half, dst in ((0, row_s), (1, col_s)):
                if half == 0:
                    step(ts(posu, pos, 4, None, ALU.logical_shift_right))
                else:
                    step(ts(posu, pos, TOPK - 1, None, ALU.bitwise_and))
                step(nc.vector.tensor_copy(posf, posu))
                for t in range(TT):
                    step(tt(pick, posf[:, t].unsqueeze(3).to_broadcast([P, PH, TOPK, TOPK]),
                            iota[:, 0:TOPK].unsqueeze(1).unsqueeze(1).to_broadcast([P, PH, TOPK, TOPK]), ALU.is_equal))
                    step(tt(pick, pick, idxf[:, t, half::2, :].unsqueeze(2).to_broadcast([P, PH, TOPK, TOPK]), ALU.mult))
                    step(nc.vector.tensor_reduce(dst[:, t].rearrange("p (h k) -> p h k", h=PH), pick, AX_X, ALU.add))
            ve.sem_inc(sel_ready, 1)
            ve.wait_ge(selT_done, 1)

            def flat(x):
                return x.rearrange("p g c -> p (g c)")

            step(nc.vector.tensor_copy(flat(rowT), bank[:, 4, :]))
            step(nc.vector.tensor_copy(flat(colT), bank[:, 5, :]))
            step(nc.vector.tensor_copy(flat(gateT), bank[:, 6, :]))
            by_pair = [x.rearrange("p (i b) c -> p b i c", b=2) for x in (rowT, colT, gateT)]

            def one_hots(j):
                for q in range(2 * TG // 4):
                    if not (isinstance(j, int) and q < 2):
                        ve.wait_ge(oh_used, 16 * j + (q - 1))
                    for x in range(4):
                        c = 4 * (q % (TG // 4)) + x
                        row, col, gate = (v[:, q // (TG // 4), j, c:c + 1] for v in by_pair)
                        ts(onehot[:, q % 2, x, 0, :], iota, row, None, ALU.is_equal)
                        ins = ts(onehot[:, q % 2, x, 1, :], iota, col, gate, ALU.is_equal, ALU.mult)
                    ins.then_inc(oh_ready, 1)

            one_hots(0)
            with ve.Fori(1, NTG // 2) as j:
                one_hots(j)
            for k in range(2):
                ve.wait_ge(p_hi_ready, k + 1)
                mark(tt(b_lo[:, 4 + k, :], pT[:, k, :], b_hi[:, 4 + k, :].bitcast(F32), ALU.subtract), p_split)

            def weigh(i, c):
                b = c // JQ
                if c % JQ == 0:
                    ve.wait_ge(gate_landed[b], 16 * i + 16)
                    ve.wait_ge(acts_landed[b], 16 * i + 16)
                tt(wgt[:, c % 2, :].rearrange("p (g t) -> p g t", g=NTG),
                   acts[:, b, c % JQ, :].rearrange("p (g t) -> p g t", g=NTG),
                   gates[:, b, :, c % JQ, :], ALU.mult).then_inc(wgt_ready, 1)
                ve.wait_ge(wgt_hi_ready, STEP * i + (c + 1))
                tt(b_lo[:, c % 4, :], wgt[:, c % 2, :], b_hi[:, c % 4, :].bitcast(F32),
                   ALU.subtract).then_inc(wgt_split, 1)

            def weigh_turn(i):
                for c in range(STEP):
                    if not (isinstance(i, int) and c < 2):
                        ve.wait_ge(wgt_split, STEP * i + (c - 1))
                    weigh(i, c)

            weigh_turn(0)
            with ve.Fori(1, NKEY // STEP) as i:
                weigh_turn(i)
            ve.wait_ge(up_done, NKEY)
            for m in range(KT):
                mark(tt(xT[:, m, :], bank[:, m, :], xT[:, m, :], ALU.add), up_added)

            norm(2)
            for m in range(KT):
                z = next_tile()
                ve.wait_ge(pproj_ready, m + 1)
                step(tt(prod, z, pproj[:, m, :], ALU.mult))
                ve.sem_inc(tile_free, 1)
                mark(tt(xT[:, m, :], xT[:, m, :], prod, ALU.add), x_ready)
            norm_scale(3)
            for k in range(KT):
                mark(stt(out=final[:, k, :], in0=xT[:, k, :], scalar=gains[:, 3, k:k + 1], in1=rrms,
                    op0=ALU.mult, op1=ALU.mult), final_ready)


def constants():
    f = np.float32

    def rope(dim):
        inv = (f(1.0) / np.power(f(10000.0), np.arange(0, dim, 2, dtype=f) / f(dim))).astype(f)
        ang = np.arange(S, dtype=f)[None, :] * inv[:, None]
        return np.cos(ang).astype(f), np.sin(ang).astype(f)

    c, s = rope(RDK)
    rope_r = np.stack([c, s], 1)
    c, s = rope(ADH)
    rope_a = np.stack([np.concatenate([c, c]), np.concatenate([-s, s])], 1)
    n = np.arange(S)[None, :] - np.arange(P)[:, None]
    decay = np.zeros((RH, P, S), f)
    for h in range(RH):
        gamma = np.log(1.0 - 2.0 ** (-5.0 - h))
        decay[h] = np.where(n >= 0, np.exp(gamma * np.maximum(n, 0)) * RDK ** -0.5, 0.0)
    q = np.arange(P)[:, None] // CHUNK
    k = np.arange(2 * P)[None, :] // CHUNK
    mask = np.zeros((P, TT, 2 * P), f)
    mask[:] = np.where((k == q + 1) | (k == q + 2), 0.0, NEG)[:, None, :]
    mask[:, 0, 0:P] = NEG
    eye = np.eye(P, dtype=f)
    fixed = np.concatenate([eye, np.roll(eye, P // 2, axis=1), np.ones((P, P), f),
                            np.broadcast_to(np.arange(P, dtype=f), (P, P))], 1)
    return rope_r, rope_a, decay, mask, fixed


def kernel(**inputs):
    import concourse.bacc as bacc
    from concourse.bass_utils import run_bass_kernel_spmd

    a = {k: np.asarray(v) for k, v in inputs.items()}
    rope_r, rope_a, decay, mask, fixed = constants()
    w_in = a["w_in"][0]

    def by_columns(w, first, n):
        return w[:, first:first + P * n].reshape(KT, P, n, P).transpose(2, 1, 0, 3).reshape(n, P, UW)

    wor = a["w_o_ret"][0].reshape(RH, 4, P, 4, 2 * P).transpose(0, 3, 2, 1, 4).reshape(4 * RH, P, UW)
    down = a["peer_down"][0].reshape(P, NKEY, KT, P).transpose(1, 3, 2, 0).reshape(NKEY, P, UW)
    up = a["peer_up"][0].reshape(P, NKEY, D).transpose(1, 0, 2)
    pp = a["w_ple_proj"][0].reshape(2, P, 2, 4 * P).transpose(2, 1, 0, 3).reshape(2, P, UW)
    kinds = {
        "aq": by_columns(w_in, AQ0, AH), "ak": by_columns(w_in, AK0, AKV), "av": by_columns(w_in, AV0, AKV),
        "rq": by_columns(w_in, RQ0, 2 * RH), "rk": by_columns(w_in, RK0, 2 * RH),
        "rv": by_columns(w_in, RV0, 4 * RH), "rg": by_columns(w_in, RG0, 4 * RH),
        "ga": by_columns(w_in, GA0, KT), "gr": by_columns(w_in, GR0, KT),
        "wor": wor, "woa": by_columns(a["w_o_att"][0], 0, KT), "out": by_columns(a["w_out"][0], 0, KT),
        "pq": by_columns(a["w_peer_query"][0], 0, 2 * PH), "dn": down, "up": up, "pp": pp,
        "pg": by_columns(a["w_ple_gate"][0], 0, KT),
    }
    weights = np.empty((NU, P, UW), np.float32)
    for n, (kind, i) in enumerate(UNITS):
        weights[n] = kinds[kind][i]

    def to_columns(x, tiles):
        return np.ascontiguousarray(x.reshape(S, tiles, P).transpose(2, 1, 0))

    gains = np.stack([a["mix_norm"][0], a["ffn_norm"][0], a["ple_norm"][0], a["final_norm"]])
    gains = gains.reshape(4, KT, P).transpose(2, 0, 1).reshape(P, 4 * KT)
    sinks = np.broadcast_to(a["attn_sinks"][0], (P, AH))
    sub_keys = a["peer_sub_keys"][0].transpose(2, 0, 1).reshape(P, 2 * NKEY)
    small = np.ascontiguousarray(np.concatenate([fixed, gains, sinks, sub_keys], 1))

    nc = bacc.Bacc("TRN2", target_bir_lowering=False, num_devices=1, dynamic_dma_scratch_size=1024)
    arrays = {
        "x_cols": to_columns(a["x"][0], KT), "weights": weights, "small_in": small, "rope_r": rope_r,
        "decay": decay, "rope_a": rope_a, "mask": mask, "p_cols": to_columns(a["p"][0, 0], 2),
    }
    args = [nc.dram_tensor(k, v.shape, F32, kind="ExternalInput").ap() for k, v in arrays.items()]
    args.append(nc.dram_tensor("outT", (P, KT, S), F32, kind="ExternalOutput").ap())
    block_program(nc, *args)
    r = run_bass_kernel_spmd(nc, [arrays], core_ids=[0])
    return r.results[0]["outT"].transpose(2, 1, 0).reshape(1, S, D)
```

```python
from contextlib import ExitStack

import numpy as np

import concourse.bass as bass
from concourse import mybir

F32 = mybir.dt.float32
F32R = mybir.dt.float32r
U32 = mybir.dt.uint32
ALU = mybir.AluOpType
ACT = mybir.ActivationFunctionType
AX_X = mybir.AxisListType.X

D, S, CHUNK, EPS = 1024, 512, 64, 1e-6
AH, AKV, ADH = 8, 2, 128
RH, RDK, RDV = 4, 256, 512
PH, NKEY, TOPK = 8, 128, 16
PLE = 256
NEG = -1e30
P = 128
KT = D // P
TT = S // P
LOWEST = -3.0e38

AQ0, AK0, AV0 = 0, AH * ADH, AH * ADH + AKV * ADH
RQ0 = AV0 + AKV * ADH
RK0, RV0 = RQ0 + RH * RDK, RQ0 + 2 * RH * RDK
RG0 = RV0 + RH * RDV
GA0 = RG0 + RH * RDV
GR0 = GA0 + D

UW = 1024
RAW = 4
RING = 8


FILLERS = [("gr", KT - 2), ("gr", KT - 1), ("ga", 0), ("ga", 1)]


def weight_units():
    u = []
    for i in range(RH):
        u += [("rq", 2 * i), ("rq", 2 * i + 1), ("rk", 2 * i), ("rk", 2 * i + 1)]
        u += [("rv", 4 * i + c) for c in range(4)]
        if i > 0:
            u += [("wor", 4 * (i - 1) + c) for c in range(4)]
        u += [("rg", 4 * i + c) for c in range(4)]
    u += [("ak", 0), ("ak", 1), ("av", 0), ("av", 1), ("gr", 0), ("gr", 1)]
    u += [("wor", 4 * (RH - 1) + c) for c in range(4)]
    u += [("gr", m) for m in range(2, KT - 2)]
    u += [("aq", h) for h in range(AH)]
    u += FILLERS
    for m in range(KT):
        u += [("woa", m)] + ([("ga", m + 2)] if m + 2 < KT else [])
    u += [("out", m) for m in range(KT)]
    u += [("pq", m) for m in range(2 * PH)]
    u += [("dn", e) for e in range(NKEY)]
    u += [("up", e) for e in range(NKEY)]
    u += [("pp", 0), ("pp", 1)]
    u += [("pg", m) for m in range(KT)]
    return u


UNITS = weight_units()
NU = len(UNITS)
UNIT = {k: n for n, k in enumerate(UNITS)}
DN0, UP0 = UNIT[("dn", 0)], UNIT[("up", 0)]
LEAD = 5


def projection_outputs():
    o = []
    for i in range(RH):
        o += [("rq", 2 * i), ("rq", 2 * i + 1), ("rk", 2 * i), ("rk", 2 * i + 1)]
        o += [("rv", i, t) for t in range(TT)]
        if i > 0:
            o += [("wor", i - 1, m) for m in range(KT)]
        o += [("rg", i, t) for t in range(TT)]
    o += [("ak", 0), ("ak", 1)] + [("av", t) for t in range(TT)] + [("gr", 0), ("gr", 1)]
    o += [("wor", RH - 1, m) for m in range(KT)]
    o += [("gr", m) for m in range(2, KT - 2)]
    o += [("aq", h) for h in range(AH)]
    o += FILLERS
    for m in range(KT):
        o += [("woa", m)] + ([("ga", m + 2)] if m + 2 < KT else [])
    o += [("out", m) for m in range(KT)]
    o += [("pq", m) for m in range(2 * PH)]
    o += [("pp", m) for m in range(KT)]
    o += [("pg", m) for m in range(KT)]
    return o


OUT = {k: n for n, k in enumerate(projection_outputs())}
LAST_UNIT = {}
for _k in OUT:
    if _k[0] in ("rv", "rg"):
        LAST_UNIT[_k] = UNIT[(_k[0], 4 * _k[1] + 3)]
    elif _k[0] == "wor":
        LAST_UNIT[_k] = UNIT[("wor", 4 * _k[1] + _k[2] // 2)]
    elif _k[0] == "av":
        LAST_UNIT[_k] = UNIT[("av", 1)]
    elif _k[0] == "pp":
        LAST_UNIT[_k] = UNIT[("pp", _k[1] // 4)]
    else:
        LAST_UNIT[_k] = UNIT[_k]
USED_AT = {}
for _k, _n in OUT.items():
    if _k[0] in ("rv", "rg"):
        _units = range(LAST_UNIT[_k] - 3, LAST_UNIT[_k] + 1)
    elif _k[0] == "av":
        _units = range(LAST_UNIT[_k] - 1, LAST_UNIT[_k] + 1)
    else:
        _units = [LAST_UNIT[_k]]
    for _u in _units:
        USED_AT[_u] = _n

S_AT = [sum(S - P * i for i in range(j)) for j in range(TT)]
SMALL = 3 * P + 4 * KT + AH + 2 * NKEY
SCRATCH = 15104

TG = 32
NTG = S // TG
JQ = 4
STEP = 8
FIRST_Z = 6
AHEAD = 2
RAW_Q = 4


def block_program(nc, xT_d, w_d, small_d, rope_r_d, decay_d, rope_a_d, mask_d, pT_d, out_d):
    gate_d = nc.dram_tensor("gate_scratch", (NTG, P, NKEY * TG), F32, kind="Internal").ap()
    act_d = nc.dram_tensor("act_scratch", (NKEY // 2, P, 2 * S), F32, kind="Internal").ap()

    with ExitStack() as ctx:
        def sb(name, shape, dt=F32):
            return ctx.enter_context(nc.sbuf_tensor(name, shape, dt))

        def sem(name):
            return ctx.enter_context(nc.semaphore(name))

        xT = sb("xT", [P, KT, S])
        raw = sb("raw", [P, RAW, UW])
        w_hi = sb("w_hi", [P, RING, UW], F32R)
        w_lo = sb("w_lo", [P, RING, UW], F32R)
        h_hi = sb("h_hi", [P, KT, S], F32R)
        h_lo = sb("h_lo", [P, KT, S], F32R)
        b_hi = sb("b_hi", [P, KT, S], F32R)
        b_lo = sb("b_lo", [P, KT, S], F32R)
        small = sb("small", [P, SMALL])
        ident, ones = small[:, 0:128], small[:, 128:256]
        iota = small[:, 256:384]
        gains = small[:, 384:416].rearrange("p (n k) -> p n k", n=4)
        sinks = small[:, 416:424]
        sub_keys = small[:, 424:680].rearrange("p (a k) -> p a k", a=2)
        misc = sb("misc", [P, 128])
        scr = sb("scr", [P, SCRATCH])

        def cut(at, n):
            assert at + n <= SCRATCH, (at, n)
            return scr[:, at:at + n]

        def cut3(at, a, b):
            return cut(at, a * b).rearrange("p (a b) -> p a b", a=a)

        yacc = cut3(0, KT, S)
        tile2 = cut3(4096, 2, S)
        prod = cut(5120, S)
        sq = cut3(8704, 2, S)
        normed = cut3(9728, 2, S)
        rrms = cut(10752, S)
        ssum = cut(11264, S)
        rms4, inv4 = misc[:, 104:108], misc[:, 108:112]
        rope_r = cut3(5632, 2, S)
        decay = cut3(6656, 2, S)
        r_q = cut3(7680, 2, S)
        r_k = cut3(8704, 2, S)
        r_v_hi, r_v_lo = b_hi[:, TT:, :], b_lo[:, TT:, :]
        r_prod = cut(9728, S)
        r_g = cut3(11776, TT, RDV)
        r_s_hi, r_s_lo = (b[:, 0:TT, :].rearrange("p a n -> p (a n)") for b in (b_hi, b_lo))
        stats = misc[:, 0:24].rearrange("p (t n) -> p t n", t=TT)
        mean_var = misc[:, 24:32].rearrange("p (t n) -> p t n", t=TT)
        var_eps, std4, rstd4 = misc[:, 32:36], misc[:, 36:40], misc[:, 40:44]
        a_k = cut3(5632, AKV, S)
        a_v = cut3(6656, TT, AKV * ADH)
        a_q = cut3(7680, 2, S)
        a_s = cut(8704, 2048).rearrange("p (b t k) -> p b t k", b=2, t=TT)
        a_pT = cut(10752, 1024).rearrange("p (t b q) -> p t b q", t=TT, b=2)
        rope_a = cut3(13824, 2, S)
        mask = cut(12800, 1024).rearrange("p (t k) -> p t k", t=TT)
        k_swap, q_swap = cut3(9728, 2, S), cut3(11776, 2, S)
        smax, negmax, psum4, esink, rden = (misc[:, 48 + 4 * n:52 + 4 * n] for n in range(5))
        s12 = cut(5632, 4096).rearrange("p (m t k) -> p m t k", m=8, t=TT)
        taken = cut(11776, 1024).rearrange("p (t k) -> p t k", t=TT)
        cand = cut(0, 1024).rearrange("p (t k) -> p t k", t=TT)
        val = cut(9728, 1024).rearrange("p (t m k) -> p t m k", t=TT, m=2 * PH)
        idx = cut(10752, 1024).bitcast(U32).rearrange("p (t m k) -> p t m k", t=TT, m=2 * PH)
        idxf = cut(5632, 1024).rearrange("p (t m k) -> p t m k", t=TT, m=2 * PH)
        top = cut(2048, 512).rearrange("p (t h k) -> p t h k", t=TT, h=PH)
        pos = cut(2560, 512).bitcast(U32).rearrange("p (t h k) -> p t h k", t=TT, h=PH)
        posu = cut(3072, 512).bitcast(U32).rearrange("p (t h k) -> p t h k", t=TT, h=PH)
        posf = cut(3584, 512).rearrange("p (t h k) -> p t h k", t=TT, h=PH)
        pick = cut(0, 2048).rearrange("p (h k j) -> p h k j", h=PH, k=TOPK)
        row_s = cut(6656, 512).rearrange("p (t n) -> p t n", t=TT)
        col_s = cut(7168, 512).rearrange("p (t n) -> p t n", t=TT)
        gate_s = cut(7680, 512).rearrange("p (t n) -> p t n", t=TT)
        gsum = misc[:, 72:104]
        stage = cut(0, 8192).rearrange("p (b j t) -> p b j t", b=2, t=TG)
        rowT, colT, gateT_lo, gateT_hi = (cut(8192 + 512 * n, S).rearrange("p (g c) -> p g c", g=NTG) for n in range(4))
        gate_r = b_lo[:, 7, :]
        onehots = [b[:, 0:6, :].rearrange("p a n -> p (a n)").rearrange("p (b n q k) -> p b n q k", b=2, q=4, n=3)
                   for b in (b_hi, b_lo)]

        def onehot(q, x, n):
            return onehots[q // 2 % 2][:, q % 2, n, x, :]

        act = cut3(13056, 4, S)
        gates = cut(0, 4096).rearrange("p (b g j t) -> p b g j t", b=2, g=NTG, j=JQ)
        acts = cut(4096, 4096).rearrange("p (b j t) -> p b j t", b=2, j=JQ)
        wgt = cut3(8192, 2, S)
        pT = cut3(10240, 2, S)
        pproj = cut3(0, KT, S)
        final = cut3(0, KT, S)

        bank = ctx.enter_context(nc.psum_tensor("bank", [P, 8, 512], F32))

        landed = [sem(f"landed{i}") for i in range(RAW)]
        hi_done = sem("hi_done")
        lo_done = sem("lo_done")
        proj_done = sem("proj_done")
        proj_free = [sem("proj_free0"), sem("proj_free1")]
        tile_ready, tile_free = sem("tile_ready"), sem("tile_free")
        x_landed = [sem(f"x_landed{i}") for i in range(KT // 2)]
        small_landed = sem("small_landed")
        rope_r_landed, rope_a_landed, p_landed = sem("rope_r_landed"), sem("rope_a_landed"), sem("p_landed")
        mask_landed = sem("mask_landed")
        decay_landed = [sem("decay_landed0"), sem("decay_landed1")]
        u_hi_ready, u_ready = sem("u_hi_ready"), sem("u_ready")
        sq_ready, sq_used, ss_done = sem("sq_ready"), sem("sq_used"), sem("ss_done")
        ms_ready, rms_ready = sem("ms_ready"), sem("rms_ready")
        inv_ready, spread_done = sem("inv_ready"), sem("spread_done")
        normed_ready = sem("normed_ready")
        h_hi_ready, h_ready = sem("h_hi_ready"), sem("h_ready")
        x_ready = sem("x_ready")
        rot_ready = sem("rot_ready")
        rs_done, rs_ready = sem("rs_done"), sem("rs_ready")
        rv_hi_ready, rv_ready, rg_ready = sem("rv_hi_ready"), sem("rv_ready"), sem("rg_ready")
        y_done = sem("y_done")
        var_ready, std_ready, gn_done = sem("var_ready"), sem("std_ready"), sem("gn_done")
        tr_done, b_hi_ready, b_ready = sem("tr_done"), sem("b_hi_ready"), sem("b_ready")
        yacc_ready = sem("yacc_ready")
        swapped, arot_done = [sem("swapped0"), sem("swapped1")], sem("arot_done")
        av_ready, sc_done, sc_read = sem("av_ready"), sem("sc_done"), sem("sc_read")
        max_ready, exp_ready, p_ready = sem("max_ready"), sem("exp_ready"), sem("p_ready")
        pt_done, pT_ready, pv_done = sem("pt_done"), sem("pT_ready"), sem("pv_done")
        qp_ready = sem("qp_ready")
        ks_done, s12_ready, s12_free = sem("ks_done"), sem("s12_ready"), sem("s12_free")
        top_ready, gexp_ready = sem("top_ready"), sem("gexp_ready")
        sel_ready, selT_done = sem("sel_ready"), sem("selT_done")
        oh_compared, oh_ready, oh_used = sem("oh_compared"), sem("oh_ready"), sem("oh_used")
        upper_staged, stage_ready = sem("upper_staged"), sem("stage_ready")
        gate_written = [sem("gate_written0"), sem("gate_written1")]
        z_done, act_ready = sem("z_done"), sem("act_ready")
        act_written = [sem("act_written0"), sem("act_written1")]
        gate_landed = [sem("gate_landed0"), sem("gate_landed1")]
        acts_landed = [sem("acts_landed0"), sem("acts_landed1")]
        wgt_ready, wgt_hi_ready, wgt_split = sem("wgt_ready"), sem("wgt_hi_ready"), sem("wgt_split")
        up_done, up_added = sem("up_done"), sem("up_added")
        p_hi_ready, p_split, pproj_ready = sem("p_hi_ready"), sem("p_split"), sem("pproj_ready")
        scaled_ready = sem("scaled_ready")
        final_ready, stored = sem("final_ready"), sem("stored")
        dve_step = sem("dve_step")

        block = ctx.enter_context(nc.Block())
        w_rounds = w_d[0:NU // RAW * RAW].rearrange("(r s) p n -> s r p n", s=RAW)
        gate_quads = gate_d.rearrange("g p (i b n) -> b i p g n", b=2, n=JQ * TG)
        act_quads = act_d.rearrange("(i b a) p n -> b i p a n", b=2, a=2)
        gate_pairs = gate_d.rearrange("(i b) p n -> b i p n", b=2)
        act_pairs = act_d.rearrange("(i a) p n -> a i p n", a=STEP // 2)

        def scattered(q):
            b = 2 + 2 * (q % 2)
            return bank[:, b:b + 2, :].rearrange("p a (t n j) -> p a t n j", t=2, n=2)

        def proj_bank(key):
            return bank[:, OUT[key] % 2, :]

        def wait_output(eng, key):
            eng.wait_ge(proj_done, OUT[key] + 1)

        def wait_used(eng, u):
            kind, e = UNITS[u]
            if kind == "dn":
                eng.wait_ge(z_done, e + 1)
            elif kind == "up":
                eng.wait_ge(up_done, e + 1)
            else:
                eng.wait_ge(proj_done, USED_AT[u] + 1)

        def free_of(key):
            return proj_free[OUT[key] % 2]

        @block.sync
        def _(sp):
            sp.dma_start(raw[:, 0, :], w_d[0]).then_inc(landed[0], 16)
            sp.dma_start(small[:, :], small_d).then_inc(small_landed, 16)
            for i in range(KT // 2):
                sp.dma_start(xT[:, 2 * i:2 * i + 2, :], xT_d[:, 2 * i:2 * i + 2, :]).then_inc(x_landed[i], 16)
            for s in range(1, RAW):
                sp.dma_start(raw[:, s, :], w_d[s]).then_inc(landed[s], 16)
            with sp.Fori(1, NU // RAW) as r:
                for s in range(RAW):
                    sp.wait_ge(lo_done, RAW * r + (s - RAW + 1))
                    sp.dma_start(raw[:, s, :], w_rounds[s][r]).then_inc(landed[s], 16)
            for u in range(NU // RAW * RAW, NU):
                sp.wait_ge(lo_done, u - RAW + 1)
                sp.dma_start(raw[:, u % RAW, :], w_d[u]).then_inc(landed[u % RAW], 16)
            for k in range(KT):
                sp.wait_ge(final_ready, k + 1)
                sp.dma_start(out_d[:, k, :], final[:, k, :]).then_inc(stored, 16)
            sp.wait_ge(stored, 16 * KT)

        @block.gpsimd
        def _(pool):
            def lower(s):
                return nc.gpsimd.tensor_tensor(w_lo[:, s, :], raw[:, s % RAW, :], w_hi[:, s, :].bitcast(F32),
                                               ALU.subtract)

            with pool.Fori(0, NU // RING) as r:
                for s in range(RING):
                    pool.wait_ge(hi_done, RING * r + (s + 1))
                    lower(s).then_inc(lo_done, 1)
            for u in range(NU // RING * RING, NU):
                pool.wait_ge(hi_done, u + 1)
                lower(u % RING).then_inc(lo_done, 1)

        @block.scalar
        def _(sc):
            ahead = [0]
            tiles = [4]

            def upper(u, u_mod):
                s = u_mod % RAW
                sc.wait_ge(landed[s], 4 * (u - s) + 16)
                if isinstance(u, int) and u >= RING:
                    wait_used(sc, u - RING)
                nc.scalar.activation(w_hi[:, u_mod, :], raw[:, s, :], ACT.Copy).then_inc(hi_done, 1)

            def run_ahead(u):
                while ahead[0] <= min(u, NU - 1):
                    upper(ahead[0], ahead[0] % RING)
                    ahead[0] += 1

            def output(key):
                run_ahead(LAST_UNIT[key] + 4)
                wait_output(sc, key)
                return proj_bank(key)

            def to_tile(key, func):
                src = output(key)
                z = tiles[0]
                tiles[0] += 1
                if z >= 2:
                    sc.wait_ge(tile_free, z - 1)
                ins = nc.scalar.activation(tile2[:, z % 2, :], src, func)
                ins.then_inc(tile_ready, 1)
                sc.wait_ge(tile_ready, z + 1)
                sc.sem_inc(free_of(key), 1)

            def swap_halves(r, dst):
                z = tile2[:, (tiles[0] - 1) % 2, :]
                for half in range(2):
                    at = slice(64 * half, 64 * half + 64)
                    other = slice(64 - 64 * half, 128 - 64 * half)
                    sc.dma_start(dst[at, r % 2, :], z[other]).then_inc(swapped[r % 2], 16)

            def square(r, k):
                if k >= 3:
                    sc.wait_ge(sq_used, (KT - 1) * r + k - 2)
                elif k > 0 and r > 0:
                    sc.wait_ge(sq_used, (KT - 1) * r)
                dst = sq[:, k % 2, :] if k else ssum
                nc.scalar.activation(dst, xT[:, k, :], ACT.Square).then_inc(sq_ready, 1)

            def gained_upper(r, k, dst):
                nc.scalar.activation(dst[:, k, :], xT[:, k, :], ACT.Copy,
                                     scale=gains[:, r, k:k + 1]).then_inc(u_hi_ready, 1)

            def root(r):
                sc.wait_ge(ms_ready, r + 1)
                nc.scalar.activation(rms4, rms4, ACT.Sqrt).then_inc(rms_ready, 1)

            def norm_upper(r, k):
                sc.wait_ge(normed_ready, KT * r + k + 1)
                nc.scalar.activation(h_hi[:, k, :], normed[:, k % 2, :], ACT.Copy).then_inc(h_hi_ready, 1)

            run_ahead(0)
            sc.wait_ge(small_landed, 16)
            for k in range(KT):
                sc.wait_ge(x_landed[k // 2], 16)
                gained_upper(0, k, b_hi)
                square(0, k)
                if k == KT // 2:
                    run_ahead(1)
            sc.dma_start(rope_r[:, :, :], rope_r_d).then_inc(rope_r_landed, 16)
            for i in range(2):
                sc.dma_start(decay[:, i, :], decay_d[i]).then_inc(decay_landed[i], 16)
            root(0)
            run_ahead(RING - 1)
            for k in range(KT):
                norm_upper(0, k)

            def transposed_upper(i, cs):
                for c in cs:
                    sc.wait_ge(tr_done, 4 * i + c + 1)
                    nc.scalar.activation(b_hi[:, c, :], bank[:, 6 + c % 2, :], ACT.Copy).then_inc(b_hi_ready, 1)

            for i in range(RH):
                if i > 0:
                    for kind in ("rq", "rk"):
                        for n in range(2):
                            to_tile((kind, 2 * i + n), ACT.Copy)
                    transposed_upper(i - 1, (0, 1))
                    if i + 1 < RH:
                        sc.wait_ge(rs_ready, 4 * i)
                        sc.dma_start(decay[:, (i + 1) % 2, :], decay_d[i + 1]).then_inc(decay_landed[(i + 1) % 2], 16)
                for t in range(TT):
                    src = output(("rv", i, t))
                    if i > 0 and t == 0:
                        sc.wait_ge(y_done, TT * i)
                    nc.scalar.activation(r_v_hi[:, t, :], src, ACT.Copy).then_inc(rv_hi_ready, 1)
                    if i > 0 and t == 0:
                        transposed_upper(i - 1, (2, 3))
                for t in range(TT):
                    src = output(("rg", i, t))
                    nc.scalar.activation(r_g[:, t, :], src, ACT.Silu).then_inc(rg_ready, 1)
                    sc.wait_ge(rg_ready, TT * i + t + 1)
                    sc.sem_inc(free_of(("rg", i, t)), 1)
                sc.wait_ge(var_ready, i + 1)
                nc.scalar.activation(std4, var_eps, ACT.Sqrt).then_inc(std_ready, 1)
            sc.dma_start(rope_a[:, :, :], rope_a_d).then_inc(rope_a_landed, 16)
            for n in range(AKV):
                to_tile(("ak", n), ACT.Copy)
                swap_halves(n, k_swap)
            for t in range(TT):
                src = output(("av", t))
                nc.scalar.activation(a_v[:, t, :], src[:, 0:AKV * ADH], ACT.Copy).then_inc(av_ready, 1)
                sc.wait_ge(av_ready, t + 1)
                sc.sem_inc(free_of(("av", t)), 1)
            transposed_upper(RH - 1, (0, 1))
            to_tile(("gr", 0), ACT.Sigmoid)
            transposed_upper(RH - 1, (2, 3))
            sc.dma_start(mask, mask_d).then_inc(mask_landed, 16)
            for m in range(1, KT - 2):
                to_tile(("gr", m), ACT.Sigmoid)

            for i in range(AH + 4):
                if i < AH:
                    to_tile(("aq", i), ACT.Copy)
                    swap_halves(AKV + i, q_swap)
                elif i < AH + 3:
                    to_tile(FILLERS[i - AH], ACT.Sigmoid)
                if 0 <= i - 2 < AH:
                    h = i - 2
                    sc.wait_ge(max_ready, h + 1)
                    for t in range(TT):
                        nc.scalar.activation(a_s[:, h % 2, t, :], a_s[:, h % 2, t, :], ACT.Exp,
                                             bias=negmax[:, t:t + 1], accum_out=psum4[:, t:t + 1])
                    nc.scalar.activation(esink, negmax, ACT.Exp, bias=sinks[:, h:h + 1]).then_inc(exp_ready, 1)
                if 0 <= i - 3 < AH:
                    h = i - 3
                    sc.wait_ge(pt_done, h + 1)
                    if h > 0:
                        sc.wait_ge(pv_done, h)
                    nc.scalar.activation(a_pT.rearrange("p t b q -> p (t b q)"),
                                         bank[:, 5:7, :].rearrange("p a b -> p (a b)"), ACT.Copy).then_inc(pT_ready, 1)
                if 0 <= i - 4 < AH:
                    h = i - 4
                    if i == AH + 3:
                        run_ahead(UNIT[FILLERS[3]] + 4)
                    sc.wait_ge(pv_done, h + 1)
                    nc.scalar.activation(b_hi[:, h, :], bank[:, 7, :], ACT.Copy).then_inc(b_hi_ready, 1)
            for m in range(1, KT):
                to_tile(("ga", m), ACT.Sigmoid)
            for m in range(KT):
                sc.wait_ge(yacc_ready, RH * KT + m + 1)
                nc.scalar.activation(h_hi[:, m, :], yacc[:, m, :], ACT.Copy).then_inc(h_hi_ready, 1)
                run_ahead(UNIT[("ga", KT - 1)] + 4 + m)
            for m in range(KT):
                run_ahead(UNIT[("out", m)] + 4)
                sc.wait_ge(x_ready, m + 1)
                gained_upper(1, m, b_hi)
                square(1, m)

            def key_scores(m):
                sc.wait_ge(ks_done, m + 1)
                if m >= 8:
                    sc.wait_ge(s12_free, m - 7)
                nc.scalar.activation(s12[:, m % 8].rearrange("p t k -> p (t k)"), bank[:, 2 + m % 2, :],
                                     ACT.Copy).then_inc(s12_ready, 1)

            run_ahead(UNIT[("pq", 0)] + 4)
            root(1)
            for k in range(KT):
                norm_upper(1, k)
                if k in (2, 6):
                    m = 1 + (k > 2)
                    run_ahead(UNIT[("pq", m)] + 4)
                    key_scores(m - 1)
            run_ahead(UNIT[("pq", RAW_Q - 1)] + 4)
            key_scores(RAW_Q - 2)
            sc.wait_ge(qp_ready, RAW_Q)
            for m in range(RAW_Q, 2 * PH):
                src = output(("pq", m))
                sc.wait_ge(ks_done, m - 1)
                nc.scalar.activation(tile2[:, m % 2, :], src, ACT.Copy).then_inc(qp_ready, 1)
                sc.wait_ge(qp_ready, m + 1)
                sc.sem_inc(free_of(("pq", m)), 1)
                key_scores(m - 1)
            key_scores(2 * PH - 1)

            run_ahead(DN0 + LEAD - 1)

            def gelu(i, c):
                e = STEP * i + c
                u = DN0 + LEAD + e
                if isinstance(i, int) and i == 0:
                    upper(u, u % RING)
                else:
                    sc.wait_ge(z_done, e - (RING - LEAD - 1))
                    upper(u, (DN0 + LEAD + c) % RING)
                sc.wait_ge(z_done, e + 1)
                if c % 2 == 0 and not (isinstance(i, int) and STEP * i + c < 4):
                    sc.wait_ge(act_written[c // 2 % 2], 32 * i + 16 * (c // 4))
                nc.scalar.activation(act[:, c % 4, :], bank[:, c % 2, :], ACT.Gelu_apprx_tanh).then_inc(act_ready, 1)
                if c % 2 == 1:
                    sc.wait_ge(act_ready, e + 1)
                    sc.dma_start(act_pairs[c // 2][i], act[:, c % 4 - 1:c % 4 + 1, :].rearrange("p a t -> p (a t)")).then_inc(
                        act_written[c // 2 % 2], 16)

            def stage_upper(j, q):
                b, t = q // (TG // 4), 4 * (q % (TG // 4))
                if t == 0 and not isinstance(j, int):
                    sc.wait_ge(gate_written[b], 16 * j)
                sc.wait_ge(oh_used, 16 * j + (q + 1))
                nc.scalar.activation(stage[:, b, :, t:t + 4].rearrange("p j (a t) -> p a t j", a=2),
                                     scattered(q)[:, :, :, 1, :], ACT.Copy).then_inc(upper_staged, 1)

            def store_gates(j, b):
                sc.wait_ge(stage_ready, 16 * j + 8 * (b + 1))
                sc.dma_start(gate_pairs[b][j], stage[:, b].rearrange("p j t -> p (j t)")).then_inc(gate_written[b], 16)

            def gelu_turn(i):
                for c in range(STEP):
                    gelu(i, c)

            def read_back(i, b):
                sc.dma_start(gates[:, b].rearrange("p g j t -> p g (j t)"), gate_quads[b][i]).then_inc(gate_landed[b], 16)
                for par in range(2):
                    sc.wait_ge(act_written[par], 32 * i + 16 * (b + 1))
                sc.dma_start(acts[:, b].rearrange("p (a j) t -> p a (j t)", a=2), act_quads[b][i]).then_inc(acts_landed[b], 16)

            def gate_turn(j):
                for c in range(STEP):
                    stage_upper(j, 2 * c)
                    gelu(j + (FIRST_Z + 1), c)
                    stage_upper(j, 2 * c + 1)
                    if c == 1 and not isinstance(j, int):
                        store_gates(j - 1, 1)
                    if c == 5:
                        store_gates(j, 0)

            gelu_turn(0)
            gelu_turn(1)
            sc.wait_ge(top_ready, 1)
            nc.scalar.activation(gate_s.rearrange("p t n -> p (t n)"), gate_s.rearrange("p t n -> p (t n)"),
                                 ACT.Exp).then_inc(gexp_ready, 1)
            with sc.Fori(2, FIRST_Z + 1) as i:
                gelu_turn(i)
            gate_turn(0)
            sc.dma_start(pT[:, :, :], pT_d).then_inc(p_landed, 16)
            with sc.Fori(1, NTG // 2) as j:
                gate_turn(j)
            store_gates(NTG // 2 - 1, 1)
            sc.wait_ge(p_landed, 16)
            sc.wait_ge(oh_used, S // 4)
            for k in range(2):
                nc.scalar.activation(b_hi[:, 6 + k, :], pT[:, k, :], ACT.Copy).then_inc(p_hi_ready, 1)

            def weight_upper(e, c):
                sc.wait_ge(wgt_ready, e + 1)
                if not isinstance(e, int) or e >= 4:
                    sc.wait_ge(up_done, e - 3)
                nc.scalar.activation(b_hi[:, c % 4, :], wgt[:, c % 2, :], ACT.Copy).then_inc(wgt_hi_ready, 1)

            def up_turn(i):
                last = isinstance(i, int) and i > 0
                for c in range(STEP):
                    e = STEP * i + c
                    if isinstance(i, int):
                        upper(UP0 + LEAD + e, (UP0 + LEAD + e) % RING)
                    else:
                        sc.wait_ge(up_done, e - (RING - LEAD - 1))
                        upper(UP0 + LEAD + e, (UP0 + LEAD + c) % RING)
                    if not last or c + AHEAD < STEP:
                        weight_upper(e + AHEAD, (c + AHEAD) % STEP)
                    if not last and c % JQ == JQ - 1:
                        sc.wait_ge(wgt_ready, e + 1)
                        read_back(i + 1, c // JQ)

            for c in range(STEP):
                if c == STEP - 1:
                    for e in range(AHEAD):
                        weight_upper(e, e)
                gelu(NKEY // STEP - 1, c)
                if c == 2:
                    for b in range(2):
                        sc.wait_ge(gate_written[b], 16 * (NTG // 2))
                    read_back(0, 0)
                    read_back(0, 1)
            up_turn(0)
            with sc.Fori(1, NKEY // STEP - 1) as i:
                up_turn(i)
            up_turn(NKEY // STEP - 1)
            ahead[0] = UP0 + NKEY + LEAD

            def embed(m):
                src = output(("pp", m))
                if m == 0:
                    sc.wait_ge(wgt_ready, NKEY)
                nc.scalar.activation(pproj[:, m, :], src, ACT.Copy).then_inc(pproj_ready, 1)
                sc.wait_ge(pproj_ready, m + 1)
                sc.sem_inc(free_of(("pp", m)), 1)

            for k in range(KT):
                sc.wait_ge(up_added, k + 1)
                gained_upper(2, k, h_hi)
                if k > 0:
                    embed(k - 1)
            embed(KT - 1)
            for k in range(KT):
                square(2, k)
            run_ahead(UNIT[("pg", 0)] + 4)
            root(2)
            for m in range(KT):
                run_ahead(UNIT[("pg", m)] + 4)
                sc.wait_ge(scaled_ready, m + 1)
                z = tile2[:, (tiles[0] + m) % 2, :]
                nc.scalar.activation(z, z, ACT.Sigmoid).then_inc(tile_ready, 1)
                sc.wait_ge(x_ready, KT + m + 1)
                square(3, m)
            root(3)

        @block.tensor
        def _(pe):
            def mm3(out, a_hi, a_lo, c_hi, c_lo, first, last):
                nc.tensor.matmul(out, a_hi, c_hi, start=first, stop=False)
                nc.tensor.matmul(out, a_hi, c_lo, start=False, stop=False)
                return nc.tensor.matmul(out, a_lo, c_hi, start=False, stop=last)

            def bank_free(key):
                n = OUT[key]
                if n >= 2:
                    pe.wait_ge(proj_free[n % 2], n // 2)

            def columns(key, r_hi, r_lo, kt=KT, u=None, at=0, width=P, tiles=None, spread_at=None):
                u = UNIT[key] if u is None else u
                pe.wait_ge(lo_done, u + 1)
                bank_free(key)
                s = u % RING
                for k in range(kt):
                    if tiles is not None:
                        pe.wait_ge(tiles[0], tiles[1] + k + 1)
                    if spread_at is not None and k == KT // 2:
                        spread(spread_at)
                    o = k * width + at
                    ins = mm3(proj_bank(key), w_hi[:, s, o:o + P], w_lo[:, s, o:o + P],
                              r_hi[:, k, :], r_lo[:, k, :], k == 0, k == kt - 1)
                ins.then_inc(proj_done, 1)

            def tokens(keys, u0, nu, ts=range(TT), tiles=None):
                pe.wait_ge(lo_done, u0 + nu)
                s = u0 % RING
                assert s + nu <= RING
                for t in ts:
                    bank_free(keys[t])
                    o = proj_bank(keys[t])[:, 0:nu * P]
                    for k in range(KT):
                        if tiles is not None and t == 0:
                            pe.wait_ge(tiles[0], tiles[1] + k + 1)
                        ins = mm3(o, h_hi[:, k, P * t:P * t + P], h_lo[:, k, P * t:P * t + P],
                                  w_hi[:, s:s + nu, k * P:k * P + P], w_lo[:, s:s + nu, k * P:k * P + P],
                                  k == 0, k == KT - 1)
                    ins.then_inc(proj_done, 1)

            def add_up(r):
                pe.wait_ge(sq_used, (KT - 1) * (r + 1))
                for t in range(TT):
                    ins = nc.tensor.matmul(bank[:, 7, t:t + 1], ssum[:, P * t:P * t + P], ones[:, 0:1],
                                           start=True, stop=True)
                ins.then_inc(ss_done, 1)

            def spread(r):
                pe.wait_ge(inv_ready, r + 1)
                for t in range(TT):
                    ins = nc.tensor.matmul(bank[:, 7, P * t:P * t + P], inv4[:, t:t + 1].to_broadcast([P, P]), ident,
                                           start=True, stop=True)
                ins.then_inc(spread_done, 1)

            def transposes(i, cs):
                pe.wait_ge(gn_done, TT * (i + 1))
                for c in cs:
                    n = 4 * i + c
                    if n >= 2:
                        pe.wait_ge(b_ready, n - 1)
                    for t in range(TT):
                        ins = nc.tensor.transpose(bank[:, 6 + c % 2, P * t:P * t + P],
                                                  r_g[:, t, P * c:P * c + P], ident)
                    ins.then_inc(tr_done, 1)

            def retention_out(i):
                pe.wait_ge(b_ready, 4 * (i + 1))
                for m in range(KT):
                    columns(("wor", i, m), b_hi, b_lo, kt=4, u=UNIT[("wor", 4 * i + m // 2)],
                            at=P * (m % 2), width=2 * P)

            pe.wait_ge(small_landed, 16)
            for i in range(RH):
                values, gates_r = [("rv", i, t) for t in range(TT)], [("rg", i, t) for t in range(TT)]
                if i == 0:
                    columns(("rq", 0), b_hi, b_lo, tiles=(u_ready, 0))
                    add_up(0)
                    columns(("rq", 1), b_hi, b_lo, spread_at=0)
                    for key in (("rk", 0), ("rk", 1)):
                        columns(key, b_hi, b_lo)
                    tokens(values, UNIT[("rv", 0)], 4, tiles=(h_ready, 0))
                else:
                    for kind in ("rq", "rk"):
                        for n in range(2):
                            columns((kind, 2 * i + n), h_hi, h_lo)
                    transposes(i - 1, (0, 1))
                    tokens(values, UNIT[("rv", 4 * i)], 4, ts=(0,))
                    transposes(i - 1, (2, 3))
                    tokens(values, UNIT[("rv", 4 * i)], 4, ts=(1, 2, 3))
                pe.wait_ge(rot_ready, 2 * i + 2)
                for j in range(TT):
                    for c in range(2):
                        ins = nc.tensor.matmul(bank[:, 2 + j, 0:S - P * j], r_k[:, c, P * j:P * j + P],
                                               r_q[:, c, P * j:S], start=c == 0, stop=c == 1)
                    ins.then_inc(rs_done, 1)
                if i > 0:
                    retention_out(i - 1)
                tokens(gates_r, UNIT[("rg", 4 * i)], 4)
                pe.wait_ge(rs_ready, TT * (i + 1))
                pe.wait_ge(rv_ready, TT * (i + 1))
                for t in range(TT):
                    for j in range(t + 1):
                        o = S_AT[j] + P * (t - j)
                        ins = mm3(bank[:, 2 + t, :], r_s_hi[:, o:o + P], r_s_lo[:, o:o + P],
                                  r_v_hi[:, j, :], r_v_lo[:, j, :], j == 0, j == t)
                    ins.then_inc(y_done, 1)
            for n in range(AKV):
                columns(("ak", n), h_hi, h_lo)
            tokens([("av", t) for t in range(TT)], UNIT[("av", 0)], AKV)
            transposes(RH - 1, (0, 1))
            columns(("gr", 0), h_hi, h_lo)
            transposes(RH - 1, (2, 3))
            columns(("gr", 1), h_hi, h_lo)
            retention_out(RH - 1)
            for m in range(2, KT - 2):
                columns(("gr", m), h_hi, h_lo)

            for i in range(AH + 4):
                if i < AH:
                    columns(("aq", i), h_hi, h_lo)
                else:
                    columns(FILLERS[i - AH], h_hi, h_lo)
                if 0 <= i - 2 < AH:
                    h = i - 2
                    kv = h // (AH // AKV)
                    pe.wait_ge(arot_done, h + 3)
                    if h > 0:
                        pe.wait_ge(sc_read, h)
                    for t in range(TT):
                        o = bank[:, 3 + t // 2, 256 * (t % 2):256 * (t % 2) + 256]
                        q = a_q[:, h % 2, P * t:P * t + P]
                        if t == 0:
                            nc.tensor.matmul(o[:, 0:P], q, a_k[:, kv, 0:P], start=True, stop=True)
                            nc.tensor.matmul(o[:, P:2 * P], q, a_k[:, kv, 0:P], start=True, stop=True)
                        else:
                            ins = nc.tensor.matmul(o, q, a_k[:, kv, P * (t - 1):P * (t + 1)], start=True, stop=True)
                    ins.then_inc(sc_done, 1)
                if 0 <= i - 3 < AH:
                    h = i - 3
                    pe.wait_ge(p_ready, h + 1)
                    if h > 0:
                        pe.wait_ge(pT_ready, h)
                    for t in range(TT):
                        for b in range(2):
                            o = ((t % 2) * 2 + b) * P
                            ins = nc.tensor.transpose(bank[:, 5 + t // 2, o:o + P],
                                                      a_s[:, h % 2, t, P * b:P * b + P], ident)
                    ins.then_inc(pt_done, 1)
                if 0 <= i - 4 < AH:
                    h = i - 4
                    kv = h // (AH // AKV)
                    pe.wait_ge(pT_ready, h + 1)
                    pe.wait_ge(av_ready, TT)
                    if h > 0:
                        pe.wait_ge(b_ready, 4 * RH + h)
                    for t in range(TT):
                        for b in range(2):
                            if t == 0 and b == 0:
                                continue
                            ins = nc.tensor.matmul(bank[:, 7, P * t:P * t + P], a_v[:, t - 1 + b, P * kv:P * kv + P],
                                                   a_pT[:, t, b, :], start=b == 0 or t == 0, stop=b == 1)
                    ins.then_inc(pv_done, 1)
            for m in range(KT):
                columns(("woa", m), b_hi, b_lo, tiles=(b_ready, 4 * RH) if m == 0 else None)
                if m + 2 < KT:
                    columns(("ga", m + 2), h_hi, h_lo)
            for m in range(KT):
                columns(("out", m), h_hi, h_lo, tiles=(h_ready, KT) if m == 0 else None)

            def key_scores(m):
                pe.wait_ge(qp_ready, m + 1)
                if m >= 2:
                    pe.wait_ge(s12_ready, m - 1)
                for t in range(TT):
                    ins = nc.tensor.matmul(bank[:, 2 + m % 2, P * t:P * t + P], tile2[:, m % 2, P * t:P * t + P],
                                           sub_keys[:, m % 2, :], start=True, stop=True)
                ins.then_inc(ks_done, 1)

            for m in range(2 * PH):
                if m < RAW_Q:
                    columns(("pq", m), b_hi, b_lo, tiles=(u_ready, KT) if m == 0 else None,
                            spread_at=1 if m == 1 else None)
                else:
                    columns(("pq", m), h_hi, h_lo, tiles=(h_ready, 2 * KT) if m == RAW_Q else None)
                if m == 0:
                    add_up(1)
                else:
                    key_scores(m - 1)
            key_scores(2 * PH - 1)

            def down(i, c, halfway=None):
                e = STEP * i + c
                pe.wait_ge(lo_done, e + (DN0 + 1))
                if isinstance(i, int) and i == 0 and c < 2:
                    pe.wait_ge(proj_free[c], (OUT[("pp", 0)] + 1 - c) // 2)
                else:
                    pe.wait_ge(act_ready, e - 1)
                s = (DN0 + c) % RING
                for k in range(KT):
                    if k == KT // 2 and halfway is not None:
                        halfway()
                    ins = mm3(bank[:, c % 2, :], w_hi[:, s, P * k:P * k + P], w_lo[:, s, P * k:P * k + P],
                              h_hi[:, k, :], h_lo[:, k, :], k == 0, k == KT - 1)
                ins.then_inc(z_done, 1)

            def down_turn(i):
                for c in range(STEP):
                    down(i, c)

            def scatter(j, q):
                pe.wait_ge(oh_ready, 16 * j + (q + 1))
                if not (isinstance(j, int) and q < 2):
                    pe.wait_ge(stage_ready, 16 * j + (q - 1))
                for x in range(4):
                    ins = nc.tensor.matmul(bank[:, 2 + 2 * (q % 2) + x // 2, 256 * (x % 2):256 * (x % 2) + 256],
                                           onehot(q, x, 0), onehot(q, x, slice(1, 3)), start=True, stop=True)
                ins.then_inc(oh_used, 1)

            def scatter_turn(j):
                for c in range(STEP):
                    down(j + (FIRST_Z + 1), c, halfway=lambda: scatter(j, 2 * c))
                    scatter(j, 2 * c + 1)

            down_turn(0)
            with pe.Fori(1, FIRST_Z) as i:
                down_turn(i)
            pe.wait_ge(s12_ready, 2 * PH)
            pe.wait_ge(sel_ready, 1)
            for n, src in enumerate((row_s, col_s, gate_s)):
                for t in range(TT):
                    ins = nc.tensor.transpose(bank[:, 4 + n, P * t:P * t + P], src[:, t, :], ident)
            ins.then_inc(selT_done, 1)
            down_turn(FIRST_Z)
            scatter_turn(0)
            with pe.Fori(1, NTG // 2) as j:
                scatter_turn(j)
            down_turn(NKEY // STEP - 1)

            pe.wait_ge(stage_ready, S // 4)

            def up(i, c):
                e = STEP * i + c
                pe.wait_ge(lo_done, e + (UP0 + 1))
                pe.wait_ge(wgt_split, e + 1)
                first = isinstance(i, int) and i == 0 and c == 0
                last = isinstance(i, int) and i > 0 and c == STEP - 1
                s = (UP0 + c) % RING
                for m in [*range(2, KT), 0, 1]:
                    if first and m == 0:
                        pe.wait_ge(act_ready, NKEY)
                    ins = mm3(bank[:, m, :], w_hi[:, s, P * m:P * m + P], w_lo[:, s, P * m:P * m + P],
                              b_hi[:, c % 4, :], b_lo[:, c % 4, :], first, last)
                ins.then_inc(up_done, 1)

            def up_turn(i):
                for c in range(STEP):
                    up(i, c)

            up_turn(0)
            with pe.Fori(1, NKEY // STEP - 1) as i:
                up_turn(i)
            up_turn(NKEY // STEP - 1)

            pe.wait_ge(up_added, 2)
            pe.wait_ge(p_split, 2)

            def embed(m):
                columns(("pp", m), b_hi[:, 6:8], b_lo[:, 4:6], kt=2, u=UNIT[("pp", m // 4)], at=P * (m % 4),
                        width=4 * P)

            for m in range(KT):
                embed(m)
            for m in range(KT):
                columns(("pg", m), h_hi, h_lo, tiles=(u_ready, 2 * KT) if m == 0 else None,
                        spread_at=2 if m == 1 else None)
                if m == 0:
                    add_up(2)
            add_up(3)
            spread(3)

        @block.vector
        def _(ve):
            steps = [0]
            tiles = [0]

            def step(ins):
                steps[0] += 1
                ins.then_inc(dve_step, 1)
                ve.wait_ge(dve_step, steps[0])

            counts = {}

            def mark(ins, signal):
                counts[signal.name] = counts.get(signal.name, 0) + 1
                ins.then_inc(signal, 1)
                ve.wait_ge(signal, counts[signal.name])

            tt, ts, stt = nc.vector.tensor_tensor, nc.vector.tensor_scalar, nc.vector.scalar_tensor_tensor

            def gained_lower(r, k, lo, hi):
                ve.wait_ge(u_hi_ready, KT * r + k + 1)
                stt(out=lo[:, k, :], in0=xT[:, k, :], scalar=gains[:, r, k:k + 1], in1=hi[:, k, :].bitcast(F32),
                    op0=ALU.mult, op1=ALU.subtract).then_inc(u_ready, 1)

            def add_square(r, k):
                if k > 0:
                    ve.wait_ge(sq_ready, KT * r + k + 1)
                    if k > 1:
                        ve.wait_ge(sq_used, (KT - 1) * r + k - 1)
                    tt(ssum, ssum, sq[:, k % 2, :], ALU.add).then_inc(sq_used, 1)

            def norm_scale(r):
                ve.wait_ge(ss_done, r + 1)
                mark(ts(rms4, bank[:, 7, 0:TT], 1.0 / D, EPS, ALU.mult, ALU.add), ms_ready)
                ve.wait_ge(rms_ready, r + 1)
                mark(nc.vector.reciprocal(inv4, rms4), inv_ready)
                ve.wait_ge(spread_done, r + 1)
                step(nc.vector.tensor_copy(rrms, bank[:, 7, :]))

            def norm(r, between):
                def scale(k):
                    mark(stt(out=normed[:, k % 2, :], in0=xT[:, k, :], scalar=gains[:, r, k:k + 1], in1=rrms,
                             op0=ALU.mult, op1=ALU.mult), normed_ready)

                scale(0)
                for k in range(KT):
                    if k + 1 < KT:
                        scale(k + 1)
                    ve.wait_ge(h_hi_ready, (KT * (r + 1) if r else 0) + k + 1)
                    mark(tt(h_lo[:, k, :], normed[:, k % 2, :], h_hi[:, k, :].bitcast(F32), ALU.subtract), h_ready)
                    if k in between:
                        between[k]()

            def next_tile():
                z = tiles[0]
                tiles[0] += 1
                ve.wait_ge(tile_ready, z + 1)
                return tile2[:, z % 2, :]

            def scaled_tile(key):
                wait_output(ve, key)
                step(tt(tile2[:, OUT[key] % 2, :], proj_bank(key), rrms, ALU.mult))
                ve.sem_inc(tile_ready, 1)
                ve.sem_inc(free_of(key), 1)

            def rotate_pair(dst):
                z1, z2 = next_tile(), next_tile()
                c, s = rope_r[:, 0, :], rope_r[:, 1, :]
                step(tt(dst[:, 0, :], z1, c, ALU.mult))
                step(tt(prod, z2, s, ALU.mult))
                step(tt(dst[:, 0, :], dst[:, 0, :], prod, ALU.subtract))
                mark(tt(prod, z1, s, ALU.mult), tile_free)
                step(tt(dst[:, 1, :], z2, c, ALU.mult))
                ve.sem_inc(tile_free, 1)
                mark(tt(dst[:, 1, :], dst[:, 1, :], prod, ALU.add), rot_ready)

            def rotate(r, dst):
                z = next_tile()
                ve.wait_ge(swapped[r % 2], 32 * (r // 2 + 1))
                step(tt(prod, (k_swap if r < AKV else q_swap)[:, r % 2, :], rope_a[:, 1, :], ALU.mult))
                step(tt(dst, z, rope_a[:, 0, :], ALU.mult))
                step(tt(dst, dst, prod, ALU.add))
                ve.sem_inc(tile_free, 1)
                ve.sem_inc(arot_done, 1)

            def transposed_lower(i, cs):
                for c in cs:
                    ve.wait_ge(b_hi_ready, 4 * i + c + 1)
                    mark(tt(b_lo[:, c, :], bank[:, 6 + c % 2, :], b_hi[:, c, :].bitcast(F32), ALU.subtract), b_ready)

            def add_retention(i):
                for m in range(KT):
                    key = ("wor", i, m)
                    wait_output(ve, key)
                    if i == 0:
                        ins = nc.vector.tensor_copy(yacc[:, m, :], proj_bank(key))
                    else:
                        ins = tt(yacc[:, m, :], proj_bank(key), yacc[:, m, :], ALU.add)
                    mark(ins, yacc_ready)
                    ve.sem_inc(free_of(key), 1)

            def gate_retention(m):
                z = next_tile()
                mark(tt(yacc[:, m, :], yacc[:, m, :], z, ALU.mult), tile_free)

            ve.wait_ge(small_landed, 16)
            for k in range(KT):
                ve.wait_ge(x_landed[k // 2], 16)
                gained_lower(0, k, b_lo, b_hi)
                add_square(0, k)
            norm_scale(0)
            scaled_tile(("rq", 0))
            scaled_tile(("rq", 1))
            ve.wait_ge(rope_r_landed, 16)
            rotate_pair(r_q)
            norm(0, {0: lambda: scaled_tile(("rk", 0)), 5: lambda: scaled_tile(("rk", 1))})
            rotate_pair(r_k)

            for i in range(RH):
                if i > 0:
                    ve.wait_ge(rs_done, TT * i)
                    rotate_pair(r_q)
                    rotate_pair(r_k)
                    transposed_lower(i - 1, range(4))
                for t in range(TT):
                    ve.wait_ge(rv_hi_ready, TT * i + t + 1)
                    mark(tt(r_v_lo[:, t, :], proj_bank(("rv", i, t)), r_v_hi[:, t, :].bitcast(F32),
                            ALU.subtract), rv_ready)
                    ve.sem_inc(free_of(("rv", i, t)), 1)
                if i > 0:
                    add_retention(i - 1)
                ve.wait_ge(decay_landed[i % 2], 16 * (i // 2 + 1))
                for j in range(TT):
                    ve.wait_ge(rs_done, TT * i + j + 1)
                    n = S - P * j
                    at = slice(S_AT[j], S_AT[j] + n)
                    step(tt(r_prod[:, 0:n], bank[:, 2 + j, 0:n], decay[:, i % 2, 0:n], ALU.mult))
                    step(nc.vector.tensor_copy(r_s_hi[:, at], r_prod[:, 0:n]))
                    mark(tt(r_s_lo[:, at], r_prod[:, 0:n], r_s_hi[:, at].bitcast(F32), ALU.subtract), rs_ready)
                for t in range(TT):
                    ve.wait_ge(y_done, TT * i + t + 1)
                    step(nc.vector.bn_stats(stats[:, t, :], bank[:, 2 + t, :]))
                    step(nc.vector.bn_aggr(mean_var[:, t, :], stats[:, t, :]))
                mark(ts(var_eps, mean_var[:, :, 1], EPS, None, ALU.add), var_ready)
                ve.wait_ge(std_ready, i + 1)
                step(nc.vector.reciprocal(rstd4, std4))
                ve.wait_ge(rg_ready, TT * (i + 1))
                for t in range(TT):
                    step(stt(out=r_g[:, t, :], in0=bank[:, 2 + t, :], scalar=mean_var[:, t, 0:1],
                             in1=r_g[:, t, :], op0=ALU.subtract, op1=ALU.mult))
                    mark(ts(r_g[:, t, :], r_g[:, t, :], rstd4[:, t:t + 1], None, ALU.mult), gn_done)
            transposed_lower(RH - 1, (0, 1))
            ve.wait_ge(rope_a_landed, 16)
            rotate(0, a_k[:, 0, :])
            transposed_lower(RH - 1, (2, 3))
            rotate(1, a_k[:, 1, :])
            add_retention(RH - 1)
            for m in range(KT - 2):
                gate_retention(m)

            ve.wait_ge(mask_landed, 16)
            for i in range(1, AH + 4):
                if 0 <= i - 2 < AH:
                    h = i - 2
                    ve.wait_ge(sc_done, h + 1)
                    if h >= 2:
                        ve.wait_ge(pt_done, h - 1)
                    step(stt(out=a_s[:, h % 2].rearrange("p t k -> p (t k)"),
                             in0=bank[:, 3:5, :].rearrange("p a b -> p (a b)"), scalar=float(ADH) ** -0.5,
                             in1=mask.rearrange("p t k -> p (t k)"), op0=ALU.mult, op1=ALU.add))
                    ve.sem_inc(sc_read, 1)
                    step(nc.vector.tensor_reduce(smax, a_s[:, h % 2], AX_X, ALU.max))
                    step(ts(smax, smax, sinks[:, h:h + 1], None, ALU.max))
                    mark(ts(negmax, smax, -1.0, None, ALU.mult), max_ready)
                if i <= AH:
                    h = i - 1
                    if h >= 2:
                        ve.wait_ge(sc_done, h - 1)
                    rotate(h + 2, a_q[:, h % 2, :])
                elif i <= AH + 2:
                    gate_retention(KT - 3 + i - AH)
                if 0 <= i - 2 < AH:
                    h = i - 2
                    ve.wait_ge(exp_ready, h + 1)
                    step(tt(rden, psum4, esink, ALU.add))
                    step(nc.vector.reciprocal(rden, rden))
                    for t in range(TT):
                        step(ts(a_s[:, h % 2, t, :], a_s[:, h % 2, t, :], rden[:, t:t + 1], None, ALU.mult))
                    ve.sem_inc(p_ready, 1)
                if 0 <= i - 4 < AH:
                    h = i - 4
                    ve.wait_ge(b_hi_ready, 4 * RH + h + 1)
                    mark(tt(b_lo[:, h, :], bank[:, 7, :], b_hi[:, h, :].bitcast(F32), ALU.subtract), b_ready)
            for m in range(KT):
                z = next_tile()
                key = ("woa", m)
                wait_output(ve, key)
                step(tt(prod, proj_bank(key), z, ALU.mult))
                ve.sem_inc(tile_free, 1)
                ve.sem_inc(free_of(key), 1)
                mark(tt(yacc[:, m, :], yacc[:, m, :], prod, ALU.add), yacc_ready)
                for n in {KT - 2: range(KT - 2), KT - 1: range(KT - 2, KT)}.get(m, ()):
                    ve.wait_ge(h_hi_ready, KT + n + 1)
                    mark(tt(h_lo[:, n, :], yacc[:, n, :], h_hi[:, n, :].bitcast(F32), ALU.subtract), h_ready)
            for m in range(KT):
                key = ("out", m)
                wait_output(ve, key)
                mark(tt(xT[:, m, :], proj_bank(key), xT[:, m, :], ALU.add), x_ready)
                ve.sem_inc(free_of(key), 1)
                if m > 0:
                    gained_lower(1, m - 1, b_lo, b_hi)
                    add_square(1, m - 1)
            gained_lower(1, KT - 1, b_lo, b_hi)
            add_square(1, KT - 1)

            def scaled_query(m):
                key = ("pq", m)
                wait_output(ve, key)
                if m >= 2:
                    ve.wait_ge(ks_done, m - 1)
                mark(tt(tile2[:, m % 2, :], proj_bank(key), rrms, ALU.mult), qp_ready)
                ve.sem_inc(free_of(key), 1)

            norm_scale(1)
            scaled_query(0)
            norm(1, {2: lambda: scaled_query(1), 6: lambda: scaled_query(2)})
            scaled_query(RAW_Q - 1)

            def together(instructions):
                for ins in instructions:
                    steps[0] += 1
                    ins().then_inc(dve_step, 1)
                ve.wait_ge(dve_step, steps[0])

            def best(lists):
                def each(f):
                    together([lambda a=a: f(*a) for a in lists])

                each(lambda src, rest, v, p: nc.vector.max(v[:, 0:8], src))
                each(lambda src, rest, v, p: nc.vector.max_index(p[:, 0:8], v[:, 0:8], src))
                each(lambda src, rest, v, p: nc.vector.match_replace(rest, v[:, 0:8], src, LOWEST))
                each(lambda src, rest, v, p: nc.vector.max(v[:, 8:16], rest))
                each(lambda src, rest, v, p: nc.vector.max_index(p[:, 8:16], v[:, 8:16], rest))

            for m in range(2 * PH):
                ve.wait_ge(s12_ready, m + 1)
                best([(s12[:, m % 8, t, :], taken[:, t, 0:P], val[:, t, m, :], idx[:, t, m, :]) for t in range(TT)])
                ve.sem_inc(s12_free, 1)
                if m % 2 == 1:
                    h = m // 2
                    together([lambda t=t: tt(cand[:, t, :].rearrange("p (a b) -> p a b", a=TOPK),
                                             val[:, t, m - 1, :].unsqueeze(2).to_broadcast([P, TOPK, TOPK]),
                                             val[:, t, m, :].unsqueeze(1).to_broadcast([P, TOPK, TOPK]), ALU.add)
                              for t in range(TT)])
                    best([(cand[:, t, :], taken[:, t, :], top[:, t, h, :], pos[:, t, h, :]) for t in range(TT)])
            g4 = gate_s.rearrange("p t (h k) -> p (t h) k", h=PH)
            top3 = top.rearrange("p t h k -> p (t h) k")
            ve.wait_ge(s12_ready, 2 * PH)
            mark(tt(g4, top3, top3[:, :, 0:1].to_broadcast([P, TT * PH, TOPK]), ALU.subtract), top_ready)
            step(nc.vector.tensor_copy(idxf, idx))
            ve.wait_ge(gexp_ready, 1)
            step(nc.vector.tensor_reduce(gsum, g4, AX_X, ALU.add))
            step(nc.vector.reciprocal(gsum, gsum))
            step(tt(g4, g4, gsum.unsqueeze(2).to_broadcast([P, TT * PH, TOPK]), ALU.mult))
            for half, dst in ((0, row_s), (1, col_s)):
                if half == 0:
                    step(ts(posu, pos, 4, None, ALU.logical_shift_right))
                else:
                    step(ts(posu, pos, TOPK - 1, None, ALU.bitwise_and))
                step(nc.vector.tensor_copy(posf, posu))
                for t in range(TT):
                    step(tt(pick, posf[:, t].unsqueeze(3).to_broadcast([P, PH, TOPK, TOPK]),
                            iota[:, 0:TOPK].unsqueeze(1).unsqueeze(1).to_broadcast([P, PH, TOPK, TOPK]), ALU.is_equal))
                    step(tt(pick, pick, idxf[:, t, half::2, :].unsqueeze(2).to_broadcast([P, PH, TOPK, TOPK]), ALU.mult))
                    step(nc.vector.tensor_reduce(dst[:, t].rearrange("p (h k) -> p h k", h=PH), pick, AX_X, ALU.add))
            ve.sem_inc(sel_ready, 1)
            ve.wait_ge(selT_done, 1)

            def flat(x):
                return x.rearrange("p g c -> p (g c)")

            step(nc.vector.tensor_copy(flat(rowT), bank[:, 4, :]))
            step(nc.vector.tensor_copy(flat(colT), bank[:, 5, :]))
            step(nc.vector.tensor_copy(gate_r, bank[:, 6, :]))
            step(nc.vector.tensor_copy(flat(gateT_hi), gate_r.bitcast(F32)))
            step(tt(flat(gateT_lo), bank[:, 6, :], flat(gateT_hi), ALU.subtract))
            keys, gates_T = (cut(at, 2 * S).rearrange("p (n i b c) -> p n i b c", n=2, i=NTG // 2, b=2)
                             for at in (8192, 9216))
            quads = TG // 4

            def four(x, j, q):
                c = 4 * (q % quads)
                return x[:, :, j, q // quads, c:c + 4].unsqueeze(3).to_broadcast([P, 2, 4, P])

            def compare(j, q):
                if not (isinstance(j, int) and 16 * j + q < 4):
                    ve.wait_ge(oh_used, 16 * j + (q - 3))
                tt(onehot(q, slice(0, 4), slice(0, 3, 2)), iota.unsqueeze(1).unsqueeze(1).to_broadcast([P, 2, 4, P]),
                   four(keys, j, q), ALU.is_equal).then_inc(oh_compared, 1)

            def times_gate(j, q):
                ve.wait_ge(oh_compared, 16 * j + (q + 1))
                col = onehot(q, slice(0, 4), 2).bitcast(F32).unsqueeze(1).to_broadcast([P, 2, 4, P])
                tt(onehot(q, slice(0, 4), slice(1, 3)), col, four(gates_T, j, q), ALU.mult).then_inc(oh_ready, 1)

            def add_parts(j, q):
                b = q // quads
                ve.wait_ge(upper_staged, 16 * j + (q + 1))
                t = 4 * (q % quads)
                dst = stage[:, b, :, t:t + 4].rearrange("p j (a t) -> p a t j", a=2)
                tt(dst, dst, scattered(q)[:, :, :, 0, :], ALU.add).then_inc(stage_ready, 1)

            def one_hots(j):
                last = isinstance(j, int) and j > 0
                for q in range(2 * quads):
                    if q + 1 < 2 * quads:
                        compare(j, q + 1)
                    elif not last:
                        compare(j + 1, 0)
                    times_gate(j, q)
                    if q >= 2:
                        add_parts(j, q - 2)
                    elif not isinstance(j, int) or last:
                        add_parts(j - 1, 2 * quads - 2 + q)

            compare(0, 0)
            one_hots(0)
            with ve.Fori(1, NTG // 2 - 1) as j:
                one_hots(j)
            one_hots(NTG // 2 - 1)
            for q in (2 * quads - 2, 2 * quads - 1):
                add_parts(NTG // 2 - 1, q)
            ve.wait_ge(oh_used, S // 4)
            for k in range(2):
                ve.wait_ge(p_hi_ready, k + 1)
                mark(tt(b_lo[:, 4 + k, :], pT[:, k, :], b_hi[:, 6 + k, :].bitcast(F32), ALU.subtract), p_split)

            def weigh(i, c):
                b = c // JQ
                if c % JQ == 0:
                    ve.wait_ge(gate_landed[b], 16 * i + 16)
                    ve.wait_ge(acts_landed[b], 16 * i + 16)
                tt(wgt[:, c % 2, :].rearrange("p (g t) -> p g t", g=NTG),
                   acts[:, b, c % JQ, :].rearrange("p (g t) -> p g t", g=NTG),
                   gates[:, b, :, c % JQ, :], ALU.mult).then_inc(wgt_ready, 1)
                ve.wait_ge(wgt_hi_ready, STEP * i + (c + 1))
                tt(b_lo[:, c % 4, :], wgt[:, c % 2, :], b_hi[:, c % 4, :].bitcast(F32),
                   ALU.subtract).then_inc(wgt_split, 1)

            def weigh_turn(i):
                for c in range(STEP):
                    if not (isinstance(i, int) and c < 2):
                        ve.wait_ge(wgt_split, STEP * i + (c - 1))
                    weigh(i, c)

            weigh_turn(0)
            with ve.Fori(1, NKEY // STEP) as i:
                weigh_turn(i)
            ve.wait_ge(up_done, NKEY)
            for m in range(KT + 2):
                if m < KT:
                    tt(xT[:, m, :], bank[:, m, :], xT[:, m, :], ALU.add).then_inc(up_added, 1)
                if m > 1:
                    gained_lower(2, m - 2, h_lo, h_hi)
            for m in range(KT):
                add_square(2, m)

            norm_scale(2)
            for m in range(KT):
                key = ("pg", m)
                wait_output(ve, key)
                mark(tt(tile2[:, tiles[0] % 2, :], proj_bank(key), rrms, ALU.mult), scaled_ready)
                ve.sem_inc(free_of(key), 1)
                z = next_tile()
                ve.wait_ge(pproj_ready, m + 1)
                step(tt(prod, z, pproj[:, m, :], ALU.mult))
                mark(tt(xT[:, m, :], xT[:, m, :], prod, ALU.add), x_ready)
                add_square(3, m)
            norm_scale(3)
            for k in range(KT):
                stt(out=final[:, k, :], in0=xT[:, k, :], scalar=gains[:, 3, k:k + 1], in1=rrms,
                    op0=ALU.mult, op1=ALU.mult).then_inc(final_ready, 1)


def constants():
    f = np.float32

    def rope(dim):
        inv = (f(1.0) / np.power(f(10000.0), np.arange(0, dim, 2, dtype=f) / f(dim))).astype(f)
        ang = np.arange(S, dtype=f)[None, :] * inv[:, None]
        return np.cos(ang).astype(f), np.sin(ang).astype(f)

    c, s = rope(RDK)
    rope_r = np.stack([c, s], 1)
    c, s = rope(ADH)
    rope_a = np.stack([np.concatenate([c, c]), np.concatenate([-s, s])], 1)
    n = np.arange(S)[None, :] - np.arange(P)[:, None]
    decay = np.zeros((RH, P, S), f)
    for h in range(RH):
        gamma = np.log(1.0 - 2.0 ** (-5.0 - h))
        decay[h] = np.where(n >= 0, np.exp(gamma * np.maximum(n, 0)) * RDK ** -0.5, 0.0)
    q = np.arange(P)[:, None] // CHUNK
    k = np.arange(2 * P)[None, :] // CHUNK
    mask = np.zeros((P, TT, 2 * P), f)
    mask[:] = np.where((k == q + 1) | (k == q + 2), 0.0, NEG)[:, None, :]
    mask[:, 0, 0:P] = NEG
    eye = np.eye(P, dtype=f)
    fixed = np.concatenate([eye, np.ones((P, P), f),
                            np.broadcast_to(np.arange(P, dtype=f), (P, P))], 1)
    return rope_r, rope_a, decay, mask, fixed


def kernel(**inputs):
    import concourse.bacc as bacc
    from concourse.bass_utils import run_bass_kernel_spmd

    a = {k: np.asarray(v) for k, v in inputs.items()}
    rope_r, rope_a, decay, mask, fixed = constants()
    w_in = a["w_in"][0]

    def by_columns(w, first, n):
        return w[:, first:first + P * n].reshape(KT, P, n, P).transpose(2, 1, 0, 3).reshape(n, P, UW)

    wor = a["w_o_ret"][0].reshape(RH, 4, P, 4, 2 * P).transpose(0, 3, 2, 1, 4).reshape(4 * RH, P, UW)
    down = a["peer_down"][0].reshape(P, NKEY, KT, P).transpose(1, 3, 2, 0).reshape(NKEY, P, UW)
    up = a["peer_up"][0].reshape(P, NKEY, D).transpose(1, 0, 2)
    pp = a["w_ple_proj"][0].reshape(2, P, 2, 4 * P).transpose(2, 1, 0, 3).reshape(2, P, UW)
    kinds = {
        "aq": by_columns(w_in, AQ0, AH), "ak": by_columns(w_in, AK0, AKV), "av": by_columns(w_in, AV0, AKV),
        "rq": by_columns(w_in, RQ0, 2 * RH), "rk": by_columns(w_in, RK0, 2 * RH),
        "rv": by_columns(w_in, RV0, 4 * RH), "rg": by_columns(w_in, RG0, 4 * RH),
        "ga": by_columns(w_in, GA0, KT), "gr": by_columns(w_in, GR0, KT),
        "wor": wor, "woa": by_columns(a["w_o_att"][0], 0, KT), "out": by_columns(a["w_out"][0], 0, KT),
        "pq": by_columns(a["w_peer_query"][0], 0, 2 * PH), "dn": down, "up": up, "pp": pp,
        "pg": by_columns(a["w_ple_gate"][0], 0, KT),
    }
    weights = np.empty((NU, P, UW), np.float32)
    for n, (kind, i) in enumerate(UNITS):
        weights[n] = kinds[kind][i]

    def to_columns(x, tiles):
        return np.ascontiguousarray(x.reshape(S, tiles, P).transpose(2, 1, 0))

    gains = np.stack([a["mix_norm"][0], a["ffn_norm"][0], a["ple_norm"][0], a["final_norm"]])
    gains = gains.reshape(4, KT, P).transpose(2, 0, 1).reshape(P, 4 * KT)
    sinks = np.broadcast_to(a["attn_sinks"][0], (P, AH))
    sub_keys = a["peer_sub_keys"][0].transpose(2, 0, 1).reshape(P, 2 * NKEY)
    small = np.ascontiguousarray(np.concatenate([fixed, gains, sinks, sub_keys], 1))

    nc = bacc.Bacc("TRN2", target_bir_lowering=False, num_devices=1, dynamic_dma_scratch_size=1024)
    arrays = {
        "x_cols": to_columns(a["x"][0], KT), "weights": weights, "small_in": small, "rope_r": rope_r,
        "decay": decay, "rope_a": rope_a, "mask": mask, "p_cols": to_columns(a["p"][0, 0], 2),
    }
    args = [nc.dram_tensor(k, v.shape, F32, kind="ExternalInput").ap() for k, v in arrays.items()]
    args.append(nc.dram_tensor("outT", (P, KT, S), F32, kind="ExternalOutput").ap())
    block_program(nc, *args)
    r = run_bass_kernel_spmd(nc, [arrays], core_ids=[0])
    return r.results[0]["outT"].transpose(2, 1, 0).reshape(1, S, D)
```
